# Optimizing a Trainium2 kernel written in Bass

```python
import math
import jax, jax.numpy as jnp
from jax import lax
import numpy as np
import functools
import jax
import jax.numpy as jnp

D_MODEL = 1024
BATCH = 1
SEQ = 512
DEPTH = 2

HEAD_DIM = 64
BLOCK = 128
A_HEADS = 8
A_KV = 2
WINDOW = 128
B_HEADS = 8
B_KV = 2
GRID_W = 64
C_WIDTH = 512
C_GROUPS = 4
C_GROUP_DIM = C_WIDTH // C_GROUPS
CHUNK = 128
N_BRANCH = 3
BRANCH_WIDTH = 512
ROPE_THETA = 10000.0
MEM_LEN = 256
X_HEADS = 4
X_HEAD_DIM = 128
X_WIDTH = X_HEADS * X_HEAD_DIM
D_FF = 2816
CONV_W = 3
ALPHA = (2 * DEPTH) ** 0.25
BETA = (8 * DEPTH) ** -0.25
LN_EPS = 1e-5
RMS_EPS = 1e-6

A_Q_W = A_HEADS * HEAD_DIM
A_KV_W = A_KV * HEAD_DIM
B_Q_W = B_HEADS * HEAD_DIM
B_KV_W = B_KV * HEAD_DIM
IN_SIZES = (A_Q_W, A_KV_W, A_KV_W, B_Q_W, B_KV_W, B_KV_W, 2 * C_WIDTH, N_BRANCH * D_MODEL)
D_IN = sum(IN_SIZES)


def _split_points(sizes):
    pts, acc = [], 0
    for s in sizes[:-1]:
        acc += s
        pts.append(acc)
    return pts

def layer_norm(x, g, b):
    xf = x.astype(jnp.float32)
    mu = jnp.mean(xf, axis=-1, keepdims=True)
    var = jnp.mean(jnp.square(xf - mu), axis=-1, keepdims=True)
    y = (xf - mu) * lax.rsqrt(var + LN_EPS) * g.astype(jnp.float32) + b.astype(jnp.float32)
    return y.astype(x.dtype)

def rms_norm(x, g):
    xf = x.astype(jnp.float32)
    y = xf * lax.rsqrt(jnp.mean(jnp.square(xf), axis=-1, keepdims=True) + RMS_EPS)
    return (y * g.astype(jnp.float32)).astype(x.dtype)

def rope(x, pos, theta):
    d = x.shape[-1]
    half = d // 2
    inv = theta ** (-jnp.arange(half, dtype=jnp.float32) * (2.0 / d))
    ang = pos.astype(jnp.float32)[:, None] * inv[None, :]
    cos = jnp.cos(ang)[:, None, :]
    sin = jnp.sin(ang)[:, None, :]
    x1 = x[..., :half].astype(jnp.float32)
    x2 = x[..., half:].astype(jnp.float32)
    out = jnp.concatenate([x1 * cos - x2 * sin, x2 * cos + x1 * sin], axis=-1)
    return out.astype(x.dtype)

def window_attention(q, k, v, sink):
    B, S, H, D = q.shape
    KV = k.shape[2]
    G = H // KV
    nb = S // BLOCK
    qb = q.reshape(B, nb, BLOCK, KV, G, D)
    pad = ((0, 0), (BLOCK, BLOCK), (0, 0), (0, 0))
    kp = jnp.pad(k, pad).reshape(B, nb + 2, BLOCK, KV, D)
    vp = jnp.pad(v, pad).reshape(B, nb + 2, BLOCK, KV, D)
    kw = jnp.concatenate([kp[:, :-2], kp[:, 1:-1], kp[:, 2:]], axis=2)
    vw = jnp.concatenate([vp[:, :-2], vp[:, 1:-1], vp[:, 2:]], axis=2)
    s = jnp.einsum('bnqkgd,bnskd->bnkgqs', qb, kw).astype(jnp.float32) / math.sqrt(D)
    blk = jnp.arange(nb, dtype=jnp.int32)[:, None]
    qpos = blk * BLOCK + jnp.arange(BLOCK, dtype=jnp.int32)[None, :]
    kpos = (blk - 1) * BLOCK + jnp.arange(3 * BLOCK, dtype=jnp.int32)[None, :]
    dist = jnp.abs(qpos[:, :, None] - kpos[:, None, :])
    valid = (dist <= WINDOW) & (kpos[:, None, :] >= 0) & (kpos[:, None, :] < S)
    s = jnp.where(valid[None, :, None, None], s, -jnp.inf)
    sink_l = jnp.broadcast_to(sink.astype(jnp.float32).reshape(KV, G)[None, None, :, :, None, None],
                              s.shape[:-1] + (1,))
    p = jax.nn.softmax(jnp.concatenate([s, sink_l], axis=-1), axis=-1)[..., :-1]
    o = jnp.einsum('bnkgqs,bnskd->bnqkgd', p.astype(v.dtype), vw)
    return o.reshape(B, S, H * D)

def dense_block_attention(q, k, v):
    B, S, H, D = q.shape
    KV = k.shape[2]
    G = H // KV
    nb = S // BLOCK
    scale = 1.0 / math.sqrt(D)
    qb = q.reshape(B, nb, BLOCK, KV, G, D).transpose(1, 0, 2, 3, 4, 5)

    def one_block(qblk):
        s = jnp.einsum('bqkgd,bskd->bkgqs', qblk, k).astype(jnp.float32) * scale
        p = jax.nn.softmax(s, axis=-1)
        return jnp.einsum('bkgqs,bskd->bqkgd', p.astype(v.dtype), v)

    o = lax.map(one_block, qb)
    return o.transpose(1, 0, 2, 3, 4, 5).reshape(B, S, H * D)

def spatial_gating(u, v, ln_g, ln_b, w_s, b_s):
    B, S, _ = v.shape
    nc = S // CHUNK
    vc = layer_norm(v, ln_g, ln_b).reshape(B, nc, CHUNK, C_GROUPS, C_GROUP_DIM)
    mixed = jnp.einsum('gij,bnjgc->bnigc', w_s, vc) + b_s.T[None, None, :, :, None]
    return u * mixed.reshape(B, S, C_WIDTH)

def hybrid_mixer(x, pos, row, col, w_in, b_gate, a_sink, b_q_gain, b_k_gain,
                 c_ln_g, c_ln_b, c_ws, c_bs, w_branch, w_mix_out):
    B, S, _ = x.shape
    proj = x @ w_in
    aq, ak, av, bq, bk, bv, cz, gate = jnp.split(proj, _split_points(IN_SIZES), axis=-1)
    aq = rope(aq.reshape(B, S, A_HEADS, HEAD_DIM), pos, ROPE_THETA)
    ak = rope(ak.reshape(B, S, A_KV, HEAD_DIM), pos, ROPE_THETA)
    av = av.reshape(B, S, A_KV, HEAD_DIM)
    out_a = window_attention(aq, ak, av, a_sink)
    half = HEAD_DIM // 2
    bq = rms_norm(bq.reshape(B, S, B_HEADS, HEAD_DIM), b_q_gain)
    bk = rms_norm(bk.reshape(B, S, B_KV, HEAD_DIM), b_k_gain)
    bq = jnp.concatenate([rope(bq[..., :half], row, ROPE_THETA), rope(bq[..., half:], col, ROPE_THETA)], axis=-1)
    bk = jnp.concatenate([rope(bk[..., :half], row, ROPE_THETA), rope(bk[..., half:], col, ROPE_THETA)], axis=-1)
    bv = bv.reshape(B, S, B_KV, HEAD_DIM)
    out_b = dense_block_attention(bq, bk, bv)
    u, v = jnp.split(jax.nn.gelu(cz, approximate=False), 2, axis=-1)
    out_c = spatial_gating(u, v, c_ln_g, c_ln_b, c_ws, c_bs)
    branches = jnp.stack([out_a, out_b, out_c], axis=2)
    gates = jax.nn.sigmoid(gate + b_gate).reshape(B, S, N_BRANCH, D_MODEL)
    merged = (jnp.einsum('bsnc,ncd->bsnd', branches, w_branch) * gates).sum(axis=2)
    return merged @ w_mix_out

def memory_cross_attention(x, mem, wq, wkv, wo):
    B, S, _ = x.shape
    M = mem.shape[1]
    q = (x @ wq).reshape(B, S, X_HEADS, X_HEAD_DIM)
    k, v = jnp.split(mem @ wkv, 2, axis=-1)
    k = k.reshape(B, M, X_HEADS, X_HEAD_DIM)
    v = v.reshape(B, M, X_HEADS, X_HEAD_DIM)
    s = jnp.einsum('bqhd,bmhd->bhqm', q, k).astype(jnp.float32) / math.sqrt(X_HEAD_DIM)
    p = jax.nn.softmax(s, axis=-1)
    o = jnp.einsum('bhqm,bmhd->bqhd', p.astype(v.dtype), v)
    return o.reshape(B, S, X_WIDTH) @ wo

def conv_ffn(x, w_up, conv_k, conv_b, w_down):
    S = x.shape[1]
    h = x @ w_up
    r = CONV_W // 2
    hp = jnp.pad(h, ((0, 0), (r, r), (0, 0)))
    h = sum(hp[:, j:j + S] * conv_k[j] for j in range(CONV_W)) + conv_b
    a, b = jnp.split(h, 2, axis=-1)
    return (jax.nn.gelu(a, approximate=False) * b) @ w_down

def first_inputs(seed: int = 0) -> dict:
    key = jax.random.key(seed)
    ks = jax.random.split(key, 26)

    def nrm(k, shape, scale):
        return jax.random.normal(k, shape, dtype=jnp.float32) * scale

    L = DEPTH
    return {
        "x": nrm(ks[0], (BATCH, SEQ, D_MODEL), 1.0),
        "mem": nrm(ks[1], (BATCH, MEM_LEN, D_MODEL), 1.0),
        "w_in": nrm(ks[2], (L, D_MODEL, D_IN), D_MODEL ** -0.5),
        "b_gate": nrm(ks[3], (L, N_BRANCH * D_MODEL), 0.1),
        "a_sink": nrm(ks[4], (L, A_HEADS), 1.0),
        "b_q_gain": 1.0 + nrm(ks[5], (L, HEAD_DIM), 0.02),
        "b_k_gain": 1.0 + nrm(ks[6], (L, HEAD_DIM), 0.02),
        "c_ln_g": 1.0 + nrm(ks[7], (L, C_WIDTH), 0.02),
        "c_ln_b": nrm(ks[8], (L, C_WIDTH), 0.02),
        "c_ws": nrm(ks[9], (L, C_GROUPS, CHUNK, CHUNK), CHUNK ** -0.5),
        "c_bs": 1.0 + nrm(ks[10], (L, C_GROUPS, CHUNK), 0.02),
        "w_branch": nrm(ks[11], (L, N_BRANCH, BRANCH_WIDTH, D_MODEL), BRANCH_WIDTH ** -0.5),
        "w_mix_out": nrm(ks[12], (L, D_MODEL, D_MODEL), BETA * D_MODEL ** -0.5),
        "ln1_g": 1.0 + nrm(ks[13], (L, D_MODEL), 0.02),
        "ln1_b": nrm(ks[14], (L, D_MODEL), 0.02),
        "x_wq": nrm(ks[15], (L, D_MODEL, X_WIDTH), D_MODEL ** -0.5),
        "x_wkv": nrm(ks[16], (L, D_MODEL, 2 * X_WIDTH), D_MODEL ** -0.5),
        "x_wo": nrm(ks[17], (L, X_WIDTH, D_MODEL), BETA * X_WIDTH ** -0.5),
        "ln2_g": 1.0 + nrm(ks[18], (L, D_MODEL), 0.02),
        "ln2_b": nrm(ks[19], (L, D_MODEL), 0.02),
        "f_w_up": nrm(ks[20], (L, D_MODEL, 2 * D_FF), D_MODEL ** -0.5),
        "f_conv_k": nrm(ks[21], (L, CONV_W, 2 * D_FF), CONV_W ** -0.5),
        "f_conv_b": nrm(ks[22], (L, 2 * D_FF), 0.02),
        "f_w_down": nrm(ks[23], (L, D_FF, D_MODEL), BETA * D_FF ** -0.5),
        "ln3_g": 1.0 + nrm(ks[24], (L, D_MODEL), 0.02),
        "ln3_b": nrm(ks[25], (L, D_MODEL), 0.02),
    }

def first_block(x, mem, w_in, b_gate, a_sink, b_q_gain, b_k_gain, c_ln_g, c_ln_b, c_ws, c_bs,
              w_branch, w_mix_out, ln1_g, ln1_b, x_wq, x_wkv, x_wo, ln2_g, ln2_b,
              f_w_up, f_conv_k, f_conv_b, f_w_down, ln3_g, ln3_b):
    seq = x.shape[1]
    rows = seq // GRID_W
    pos = jnp.arange(seq, dtype=jnp.int32)
    row = jnp.repeat(jnp.arange(rows, dtype=jnp.int32), GRID_W)
    col = jnp.tile(jnp.arange(GRID_W, dtype=jnp.int32), rows)
    for l in range(DEPTH):
        h = hybrid_mixer(x, pos, row, col, w_in[l], b_gate[l], a_sink[l], b_q_gain[l], b_k_gain[l],
                         c_ln_g[l], c_ln_b[l], c_ws[l], c_bs[l], w_branch[l], w_mix_out[l])
        x = layer_norm(ALPHA * x + h, ln1_g[l], ln1_b[l])
        h = memory_cross_attention(x, mem, x_wq[l], x_wkv[l], x_wo[l])
        x = layer_norm(ALPHA * x + h, ln2_g[l], ln2_b[l])
        h = conv_ffn(x, f_w_up[l], f_conv_k[l], f_conv_b[l], f_w_down[l])
        x = layer_norm(ALPHA * x + h, ln3_g[l], ln3_b[l])
    return x


EPS = 1e-6
D_FF_2 = 4 * D_MODEL
N_EVEN = (DEPTH + 1) // 2
N_ODD = DEPTH // 2
BLOCK_Q = 128

REL_BUCKETS = 32
REL_MAX_DIST = 128
N_BIAS_HEADS = 8

SSD_D_INNER = D_MODEL
SSD_HEAD_DIM = 64
SSD_HEADS = SSD_D_INNER // SSD_HEAD_DIM
SSD_GROUPS = 4
SSD_STATE = 128
SSD_CONV = 4
SSD_CONV_CH = SSD_D_INNER + 2 * SSD_GROUPS * SSD_STATE

DIFF_HEADS = N_BIAS_HEADS
DIFF_HEAD_DIM = D_MODEL // (2 * DIFF_HEADS)
DIFF_QK = DIFF_HEADS * 2 * DIFF_HEAD_DIM
DIFF_V = DIFF_HEADS * 2 * DIFF_HEAD_DIM

EVEN_SPLITS = (SSD_D_INNER, SSD_CONV_CH, SSD_HEADS, DIFF_QK, DIFF_QK, DIFF_V)
EVEN_IN = sum(EVEN_SPLITS)
EVEN_MIX = SSD_D_INNER + DIFF_V

RET_HEADS = 4
RET_QK_DIM = 128
RET_V_DIM = 256
ROPE_BASE = 10000.0

SWA_HEADS = N_BIAS_HEADS
SWA_KV_HEADS = 2
SWA_HEAD_DIM = 64

ODD_SPLITS = (RET_HEADS * RET_QK_DIM, RET_HEADS * RET_QK_DIM, RET_HEADS * RET_V_DIM,
              RET_HEADS * RET_V_DIM, SWA_HEADS * SWA_HEAD_DIM,
              SWA_KV_HEADS * SWA_HEAD_DIM, SWA_KV_HEADS * SWA_HEAD_DIM)
ODD_IN = sum(ODD_SPLITS)
ODD_MIX = RET_HEADS * RET_V_DIM + SWA_HEADS * SWA_HEAD_DIM


def rms_norm_2(x, w=None):
    x32 = x.astype(jnp.float32)
    y = x32 * lax.rsqrt(jnp.mean(x32 * x32, axis=-1, keepdims=True) + EPS)
    if w is not None:
        y = y * w.astype(jnp.float32)
    return y.astype(x.dtype)

def split_cols(a, sizes):
    return jnp.split(a, np.cumsum(sizes)[:-1].tolist(), axis=-1)

def t5_bucket(dist):
    dist = jnp.maximum(dist, 0)
    max_exact = REL_BUCKETS // 2
    logd = jnp.log(jnp.maximum(dist, 1).astype(jnp.float32) / max_exact)
    large = max_exact + (logd / math.log(REL_MAX_DIST / max_exact)
                         * (REL_BUCKETS - max_exact)).astype(jnp.int32)
    large = jnp.minimum(large, REL_BUCKETS - 1)
    return jnp.where(dist < max_exact, dist, large)

def scan_chunk_states(chunk_states, chunk_decay):
    def step(carry, inp):
        st, dec = inp
        return carry * dec + st, carry
    init = jnp.zeros_like(chunk_states[:, 0])
    _, prev = lax.scan(step, init, (jnp.moveaxis(chunk_states, 1, 0), jnp.moveaxis(chunk_decay, 1, 0)))
    return jnp.moveaxis(prev, 0, 1)

def causal_depthwise_conv(x, w, b):
    ch = x.shape[-1]
    out = lax.conv_general_dilated(x, w[:, None, :].astype(x.dtype), window_strides=(1,),
                                   padding=[(SSD_CONV - 1, 0)],
                                   dimension_numbers=("NWC", "WIO", "NWC"),
                                   feature_group_count=ch)
    return out + b.astype(x.dtype)

def ssd_chunked(xh, dt, A, Bg, Cg):
    b, s, h, p = xh.shape
    g, n = Bg.shape[-2:]
    r = h // g
    nc = s // CHUNK
    X = (xh * dt[..., None]).reshape(b, nc, CHUNK, g, r, p)
    Bc = Bg.reshape(b, nc, CHUNK, g, n)
    Cc = Cg.reshape(b, nc, CHUNK, g, n)
    a_cs = jnp.cumsum((dt * A).reshape(b, nc, CHUNK, g, r), axis=2)
    causal = jnp.tril(jnp.ones((CHUNK, CHUNK), dtype=bool))
    seg = a_cs[:, :, :, None] - a_cs[:, :, None, :]
    decay_in = jnp.exp(jnp.where(causal[:, :, None, None], seg, -jnp.inf))
    cb = jnp.einsum("bclgn,bcsgn->bclsg", Cc, Bc)
    y_diag = jnp.einsum("bclsg,bclsgr,bcsgrp->bclgrp", cb, decay_in, X)
    decay_to_end = jnp.exp(a_cs[:, :, -1:] - a_cs)
    chunk_states = jnp.einsum("bcsgn,bcsgr,bcsgrp->bcgrpn", Bc, decay_to_end, X)
    state_prev = scan_chunk_states(chunk_states, jnp.exp(a_cs[:, :, -1])[..., None, None])
    y_off = jnp.einsum("bclgn,bcgrpn,bclgr->bclgrp", Cc, state_prev, jnp.exp(a_cs))
    return (y_diag + y_off).reshape(b, s, h, p)

def ssd_mixer(z, xbc, dt_raw, conv_w, conv_b, dt_bias, A_log, D_skip, norm_w):
    b, s, _ = z.shape
    xbc = jax.nn.silu(causal_depthwise_conv(xbc, conv_w, conv_b))
    xs, Bs, Cs = split_cols(xbc, (SSD_D_INNER, SSD_GROUPS * SSD_STATE, SSD_GROUPS * SSD_STATE))
    xh = xs.astype(jnp.float32).reshape(b, s, SSD_HEADS, SSD_HEAD_DIM)
    dt = jax.nn.softplus(dt_raw.astype(jnp.float32) + dt_bias.astype(jnp.float32))
    A = -jnp.exp(A_log.astype(jnp.float32))
    y = ssd_chunked(xh, dt, A,
                    Bs.astype(jnp.float32).reshape(b, s, SSD_GROUPS, SSD_STATE),
                    Cs.astype(jnp.float32).reshape(b, s, SSD_GROUPS, SSD_STATE))
    y = y + xh * D_skip.astype(jnp.float32)[:, None]
    y = y.reshape(b, s, SSD_D_INNER) * jax.nn.silu(z.astype(jnp.float32))
    return rms_norm_2(y, norm_w).astype(z.dtype)

def diff_attention(q, k, v, lam, subln_w, rel_bias, layer_idx):
    b, s = q.shape[:2]
    lam_init = 0.8 - 0.6 * math.exp(-0.3 * layer_idx)
    lam32 = lam.astype(jnp.float32)
    lam_full = (jnp.exp(jnp.sum(lam32[0] * lam32[1])) - jnp.exp(jnp.sum(lam32[2] * lam32[3])) + lam_init)
    q32 = q.astype(jnp.float32) * DIFF_HEAD_DIM ** -0.5
    k32 = k.astype(jnp.float32)
    v32 = v.astype(jnp.float32)
    nb = s // BLOCK_Q
    q_blocks = jnp.moveaxis(q32.reshape(b, nb, BLOCK_Q, DIFF_HEADS, 2, DIFF_HEAD_DIM), 1, 0)
    key_pos = jnp.arange(s)

    def one_block(args):
        q_blk, blk = args
        dist = (blk * BLOCK_Q + jnp.arange(BLOCK_Q))[:, None] - key_pos[None, :]
        bias = jnp.transpose(rel_bias[t5_bucket(dist)], (2, 0, 1)).astype(jnp.float32)
        logits = jnp.einsum("bqhmd,bkhmd->bhmqk", q_blk, k32) + bias[None, :, None]
        logits = jnp.where(dist >= 0, logits, -jnp.inf)
        p = jax.nn.softmax(logits, axis=-1)
        attn = p[:, :, 0] - lam_full * p[:, :, 1]
        return jnp.einsum("bhqk,bkhe->bqhe", attn, v32)

    out = lax.map(one_block, (q_blocks, jnp.arange(nb)))
    out = jnp.moveaxis(out, 0, 1).reshape(b, s, DIFF_HEADS, 2 * DIFF_HEAD_DIM)
    out = rms_norm_2(out, subln_w) * (1.0 - lam_init)
    return out.reshape(b, s, DIFF_V).astype(q.dtype)

def rope_2(t, pos):
    half = t.shape[-1] // 2
    inv = ROPE_BASE ** (-jnp.arange(half, dtype=jnp.float32) / half)
    ang = pos[:, None] * inv[None]
    cos = jnp.cos(ang)[None, :, None]
    sin = jnp.sin(ang)[None, :, None]
    t1, t2 = t[..., :half], t[..., half:]
    return jnp.concatenate([t1 * cos - t2 * sin, t1 * sin + t2 * cos], axis=-1)

def retention(q, k, v):
    b, s = q.shape[:2]
    nc = s // CHUNK
    pos = jnp.arange(s, dtype=jnp.float32)
    Q = rope_2(q.astype(jnp.float32), pos).reshape(b, nc, CHUNK, RET_HEADS, RET_QK_DIM)
    K = (rope_2(k.astype(jnp.float32), pos) * RET_QK_DIM ** -0.5).reshape(b, nc, CHUNK, RET_HEADS, RET_QK_DIM)
    V = v.astype(jnp.float32).reshape(b, nc, CHUNK, RET_HEADS, RET_V_DIM)
    log_gamma = jnp.log(1.0 - 2.0 ** (-5.0 - jnp.arange(RET_HEADS, dtype=jnp.float32)))
    idx = jnp.arange(CHUNK, dtype=jnp.float32)
    rel = idx[:, None] - idx[None, :]
    decay_mat = jnp.where(rel >= 0, jnp.exp(jnp.maximum(rel, 0.0)[None] * log_gamma[:, None, None]), 0.0)
    scores = jnp.einsum("bclhd,bcshd->bchls", Q, K) * decay_mat
    inner = jnp.einsum("bchls,bcshe->bclhe", scores, V)
    zeta = jnp.exp((CHUNK - 1 - idx)[None] * log_gamma[:, None])
    kv = jnp.einsum("bcshd,hs,bcshe->bchde", K, zeta, V)
    chunk_decay = jnp.broadcast_to(jnp.exp(CHUNK * log_gamma)[:, None, None], (b, nc, RET_HEADS, 1, 1))
    state_prev = scan_chunk_states(kv, chunk_decay)
    xi = jnp.exp((idx + 1.0)[None] * log_gamma[:, None])
    cross = jnp.einsum("bclhd,bchde,hl->bclhe", Q, state_prev, xi)
    out = (inner + cross).reshape(b, s, RET_HEADS, RET_V_DIM)
    return rms_norm_2(out).reshape(b, s, RET_HEADS * RET_V_DIM)

def sliding_window_attention(q, k, v, sinks, rel_bias):
    b, s = q.shape[:2]
    rep = SWA_HEADS // SWA_KV_HEADS
    nb = s // BLOCK_Q
    q32 = q.astype(jnp.float32).reshape(b, nb, BLOCK_Q, SWA_KV_HEADS, rep, SWA_HEAD_DIM) * SWA_HEAD_DIM ** -0.5

    def band(t):
        t = jnp.pad(t.astype(jnp.float32), ((0, 0), (BLOCK_Q, 0), (0, 0), (0, 0)))
        t = t.reshape(b, nb + 1, BLOCK_Q, SWA_KV_HEADS, SWA_HEAD_DIM)
        return jnp.concatenate([t[:, :-1], t[:, 1:]], axis=2)

    kb, vb = band(k), band(v)
    q_off = jnp.arange(BLOCK_Q)
    k_off = jnp.arange(2 * BLOCK_Q) - BLOCK_Q
    dist = q_off[:, None] - k_off[None, :]
    k_pos = (jnp.arange(nb) * BLOCK_Q)[:, None] + k_off[None, :]
    valid = ((dist >= 0) & (dist < WINDOW))[None] & (k_pos >= 0)[:, None, :]
    bias = jnp.transpose(rel_bias[t5_bucket(dist)], (2, 0, 1)).astype(jnp.float32)
    bias = bias.reshape(SWA_KV_HEADS, rep, BLOCK_Q, 2 * BLOCK_Q)
    logits = jnp.einsum("bnqgrd,bnkgd->bngrqk", q32, kb) + bias
    logits = jnp.where(valid[None, :, None, None], logits, -jnp.inf)
    sink = jnp.broadcast_to(sinks.astype(jnp.float32).reshape(1, 1, SWA_KV_HEADS, rep, 1, 1),
                            logits.shape[:-1] + (1,))
    p = jax.nn.softmax(jnp.concatenate([logits, sink], axis=-1), axis=-1)[..., :-1]
    out = jnp.einsum("bngrqk,bnkgd->bnqgrd", p, vb)
    return out.reshape(b, s, SWA_HEADS * SWA_HEAD_DIM).astype(q.dtype)

def even_mixer(h, w_in, conv_w, conv_b, dt_bias, A_log, D_skip, ssd_norm, lam, diff_norm, w_out,
               rel_bias, layer_idx):
    b, s, _ = h.shape
    z, xbc, dt_raw, q, k, v = split_cols(h @ w_in, EVEN_SPLITS)
    y_ssd = ssd_mixer(z, xbc, dt_raw, conv_w, conv_b, dt_bias, A_log, D_skip, ssd_norm)
    y_diff = diff_attention(q.reshape(b, s, DIFF_HEADS, 2, DIFF_HEAD_DIM),
                            k.reshape(b, s, DIFF_HEADS, 2, DIFF_HEAD_DIM),
                            v.reshape(b, s, DIFF_HEADS, 2 * DIFF_HEAD_DIM),
                            lam, diff_norm, rel_bias, layer_idx)
    return jnp.concatenate([y_ssd, y_diff], axis=-1) @ w_out

def odd_mixer(h, w_in, sinks, w_out, rel_bias):
    b, s, _ = h.shape
    rq, rk, rv, rg, sq, sk, sv = split_cols(h @ w_in, ODD_SPLITS)
    y_ret = retention(rq.reshape(b, s, RET_HEADS, RET_QK_DIM),
                      rk.reshape(b, s, RET_HEADS, RET_QK_DIM),
                      rv.reshape(b, s, RET_HEADS, RET_V_DIM))
    y_ret = (y_ret * jax.nn.silu(rg.astype(jnp.float32))).astype(h.dtype)
    y_swa = sliding_window_attention(sq.reshape(b, s, SWA_HEADS, SWA_HEAD_DIM),
                                     sk.reshape(b, s, SWA_KV_HEADS, SWA_HEAD_DIM),
                                     sv.reshape(b, s, SWA_KV_HEADS, SWA_HEAD_DIM),
                                     sinks, rel_bias)
    return jnp.concatenate([y_ret, y_swa], axis=-1) @ w_out

def squared_relu_mlp(h, w1, w2):
    return jnp.square(jax.nn.relu(h @ w1)) @ w2

def sandwich(x, c_act, sublayer, g_pre, g_post, w_mod, b_mod):
    shift, scale, gate = jnp.split(c_act @ w_mod + b_mod, 3, axis=-1)
    h = rms_norm_2(x, g_pre) * (1 + scale[:, None]) + shift[:, None]
    return x + gate[:, None] * rms_norm_2(sublayer(h), g_post)

def second_inputs(seed: int = 0) -> dict:
    key = jax.random.key(seed)
    ks = jax.random.split(key, 24)

    def nrm(k, shape, scale):
        return jax.random.normal(k, shape, jnp.float32) * scale

    dt0 = jnp.exp(jax.random.uniform(ks[11], (N_EVEN, SSD_HEADS), jnp.float32,
                                     minval=math.log(1e-3), maxval=math.log(1e-1)))
    return {
        "x": nrm(ks[0], (BATCH, SEQ, D_MODEL), 1.0),
        "c": nrm(ks[1], (BATCH, D_MODEL), 1.0),
        "rel_bias": nrm(ks[2], (REL_BUCKETS, N_BIAS_HEADS), 0.5),
        "norm_gains": 1.0 + nrm(ks[3], (DEPTH, 4, D_MODEL), 0.05),
        "mod_w": nrm(ks[4], (DEPTH, 2, D_MODEL, 3 * D_MODEL), D_MODEL ** -0.5),
        "mod_b": nrm(ks[5], (DEPTH, 2, 3 * D_MODEL), 0.02),
        "mlp_w1": nrm(ks[6], (DEPTH, D_MODEL, D_FF_2), D_MODEL ** -0.5),
        "mlp_w2": nrm(ks[7], (DEPTH, D_FF_2, D_MODEL), D_FF_2 ** -0.5),
        "e_w_in": nrm(ks[8], (N_EVEN, D_MODEL, EVEN_IN), D_MODEL ** -0.5),
        "e_conv_w": nrm(ks[9], (N_EVEN, SSD_CONV, SSD_CONV_CH), SSD_CONV ** -0.5),
        "e_conv_b": nrm(ks[10], (N_EVEN, SSD_CONV_CH), 0.02),
        "e_dt_bias": dt0 + jnp.log(-jnp.expm1(-dt0)),
        "e_A_log": jnp.log(jax.random.uniform(ks[12], (N_EVEN, SSD_HEADS), jnp.float32, minval=1.0, maxval=16.0)),
        "e_D": 1.0 + nrm(ks[13], (N_EVEN, SSD_HEADS), 0.05),
        "e_ssd_norm": 1.0 + nrm(ks[14], (N_EVEN, SSD_D_INNER), 0.05),
        "e_lambda": nrm(ks[15], (N_EVEN, 4, DIFF_HEAD_DIM), 0.1),
        "e_diff_norm": 1.0 + nrm(ks[16], (N_EVEN, 2 * DIFF_HEAD_DIM), 0.05),
        "e_w_out": nrm(ks[17], (N_EVEN, EVEN_MIX, D_MODEL), EVEN_MIX ** -0.5),
        "o_w_in": nrm(ks[18], (N_ODD, D_MODEL, ODD_IN), D_MODEL ** -0.5),
        "o_sinks": nrm(ks[19], (N_ODD, SWA_HEADS), 0.5),
        "o_w_out": nrm(ks[20], (N_ODD, ODD_MIX, D_MODEL), ODD_MIX ** -0.5),
    }

def second_block(x, c, rel_bias, norm_gains, mod_w, mod_b, mlp_w1, mlp_w2, e_w_in, e_conv_w, e_conv_b,
              e_dt_bias, e_A_log, e_D, e_ssd_norm, e_lambda, e_diff_norm, e_w_out, o_w_in, o_sinks,
              o_w_out):
    c_act = jax.nn.silu(c)
    for layer in range(DEPTH):
        j = layer // 2
        if layer % 2 == 0:
            mixer = functools.partial(even_mixer, w_in=e_w_in[j], conv_w=e_conv_w[j], conv_b=e_conv_b[j],
                                      dt_bias=e_dt_bias[j], A_log=e_A_log[j], D_skip=e_D[j],
                                      ssd_norm=e_ssd_norm[j], lam=e_lambda[j], diff_norm=e_diff_norm[j],
                                      w_out=e_w_out[j], rel_bias=rel_bias, layer_idx=layer)
        else:
            mixer = functools.partial(odd_mixer, w_in=o_w_in[j], sinks=o_sinks[j], w_out=o_w_out[j],
                                      rel_bias=rel_bias)
        x = sandwich(x, c_act, mixer, norm_gains[layer, 0], norm_gains[layer, 1],
                     mod_w[layer, 0], mod_b[layer, 0])
        mlp = functools.partial(squared_relu_mlp, w1=mlp_w1[layer], w2=mlp_w2[layer])
        x = sandwich(x, c_act, mlp, norm_gains[layer, 2], norm_gains[layer, 3],
                     mod_w[layer, 1], mod_b[layer, 1])
    return x


def setup_inputs(seed=0):
    out = dict(first_inputs(seed))
    for name, value in second_inputs(seed + 1).items():
        if name != "x":
            out[name + "_2"] = value
    return out


def reference(
    x, mem, w_in, b_gate, a_sink, b_q_gain, b_k_gain, c_ln_g, c_ln_b, c_ws, c_bs, w_branch,
    w_mix_out, ln1_g, ln1_b, x_wq, x_wkv, x_wo, ln2_g, ln2_b, f_w_up, f_conv_k, f_conv_b,
    f_w_down, ln3_g, ln3_b, c_2, rel_bias_2, norm_gains_2, mod_w_2, mod_b_2, mlp_w1_2, mlp_w2_2,
    e_w_in_2, e_conv_w_2, e_conv_b_2, e_dt_bias_2, e_A_log_2, e_D_2, e_ssd_norm_2, e_lambda_2,
    e_diff_norm_2, e_w_out_2, o_w_in_2, o_sinks_2, o_w_out_2,
):
    x = first_block(
        x, mem, w_in, b_gate, a_sink, b_q_gain, b_k_gain, c_ln_g, c_ln_b, c_ws, c_bs, w_branch,
        w_mix_out, ln1_g, ln1_b, x_wq, x_wkv, x_wo, ln2_g, ln2_b, f_w_up, f_conv_k, f_conv_b,
        f_w_down, ln3_g, ln3_b,
    )
    return second_block(
        x, c_2, rel_bias_2, norm_gains_2, mod_w_2, mod_b_2, mlp_w1_2, mlp_w2_2, e_w_in_2,
        e_conv_w_2, e_conv_b_2, e_dt_bias_2, e_A_log_2, e_D_2, e_ssd_norm_2, e_lambda_2,
        e_diff_norm_2, e_w_out_2, o_w_in_2, o_sinks_2, o_w_out_2,
    )


_drawn_inputs = setup_inputs


def setup_inputs(seed=0):
    import zlib

    import numpy as np

    out = dict(_drawn_inputs(seed))
    spreads = {}
    factors = {'b_gate': 4.392,
     'a_sink': 24.671,
     'b_q_gain': 8.0,
     'b_k_gain': 8.0,
     'c_ln_g': 8.0,
     'c_ln_b': 8.0,
     'c_bs': 8.0,
     'f_conv_b': 4.881,
     'e_conv_b_2': 5.837,
     'e_D_2': 16.477,
     'o_sinks_2': 8.0}
    for name, (base, spread) in spreads.items():
        noise = np.random.default_rng([zlib.crc32(name.encode()), seed]).standard_normal(out[name].shape)
        drawn = base * np.exp(spread * noise) if base else spread * noise
        out[name] = jnp.asarray(drawn.astype(out[name].dtype))
    for name, factor in factors.items():
        out[name] = (out[name] * factor).astype(out[name].dtype)
    return out
```

```python
from contextlib import ExitStack
import math

import numpy as np

import concourse.bass as bass
from concourse import mybir

ALU = mybir.AluOpType
ACT = mybir.ActivationFunctionType
AX = mybir.AxisListType.X
F32 = mybir.dt.float32
F32R = mybir.dt.float32r
ds = bass.ds

P = 128
S = 512
D = 1024
KD = D // P
NB = S // P
DEPTH = 2
D_IN = 5632
GATE0 = 2560
D_FF = 2816
MEM = 256
ALPHA = (2 * DEPTH) ** 0.25
EVEN_IN = 6160
ODD_IN = 3840
NEG = -1.0e30
WMAX = 12
WRING = 2
HRING = 2
TT = 22
RT = 24
LAM_INIT = 0.8 - 0.6 * math.exp(0.0)
CONSTS = ["ident", "ones", "mean", "pair", "rotA", "rotB", "rotC", "dup0", "dup1", "tri", "flip"]


def constants():
    i = np.arange(P)
    c = {"ident": np.eye(P), "ones": np.ones((P, P)), "mean": np.full((P, P), 1.0 / D),
         "pair": (i[:, None] // 64 == i[None] // 64) / 64.0, "tri": (i[:, None] <= i[None]) * 1.0, "flip": np.eye(P)[::-1]}
    for name, half in (("rotA", 32), ("rotB", 16), ("rotC", 64)):
        m = np.zeros((P, P))
        for o in range(P):
            if o % (2 * half) < half:
                m[o + half, o] = -1.0
            else:
                m[o - half, o] = 1.0
        c[name] = m
    for g in range(2):
        c[f"dup{g}"] = (i[:, None] == 64 * g + i[None] % 64) * 1.0
    mats = np.stack([c[n] for n in CONSTS], 1).astype(np.float32)
    pos = np.arange(S, dtype=np.float32)
    f = np.float32

    def table(d, parts, where):
        half = d // 2
        inv = f(10000.0) ** (-np.arange(half, dtype=np.float32) * f(2.0 / d))
        ang = np.stack([where(p) * inv[p % d % half] for p in range(parts)]).astype(np.float32)
        return np.cos(ang).astype(f), np.sin(ang).astype(f)

    row, col = np.floor(pos / 64).astype(f), (pos % 64).astype(f)
    ropes = []
    ropes += table(64, P, lambda p: pos)
    ropes += table(32, P, lambda p: row if p % 64 < 32 else col)
    ropes += table(128, P, lambda p: pos)
    ropes = np.stack(ropes, 1)
    band = np.zeros((P, 3 * P), np.float32)
    j = np.arange(3 * P)
    band[np.abs(i[:, None] - (j[None] - P)) > P] = NEG
    diag = np.where(i[None] >= i[:, None], 0.0, NEG).astype(np.float32)
    dist = 511 - np.arange(640)
    dpos = np.maximum(dist, 0)
    logd = np.log(np.maximum(dpos, 1).astype(f) / f(16)) / f(math.log(8.0)) * f(16)
    bucket = np.where(dpos < 16, dpos, np.minimum(16 + logd.astype(np.int32), 31))
    onehot = (np.arange(32)[:, None] == bucket[None]).astype(f)
    bmask = np.zeros((2, 8, 640), f)
    bmask[:, :, dist < 0] = NEG
    bmask[1, :, dist >= 128] = NEG
    lg = np.log(1.0 - 2.0 ** (-5.0 - np.arange(4)))
    rel = np.arange(S)[None] - i[:, None]
    decay = np.where(rel >= 0, np.exp(np.maximum(rel, 0)[None] * lg[:, None, None]), 0.0).astype(f)
    return {"mats": mats, "ropes": ropes, "band": band, "diag": diag, "onehot": onehot, "bmask": bmask,
            "decay": decay}


class Seen:

    def __init__(self, eng, name, sems):
        self.eng, self.reg, self.step = eng, {}, {}
        for sem_name, sem, step in sems:
            r = eng.alloc_register(f"seen_{sem_name}_{name}")
            eng.reg_mov(r, 0)
            self.reg[sem_name] = r
            self.step[sem_name] = step

    def __call__(self, sem_name, times=1):
        r = self.reg[sem_name]
        self.eng.reg_add(r, r, self.step[sem_name] * times)
        return r


def build(nc, a, out, bias_dram):
    ctx = ExitStack()
    with ctx:
        def sb(name, shape, dt=F32):
            return ctx.enter_context(nc.sbuf_tensor(name, shape, dt))

        W32 = sb("w_raw", [P, WRING, WMAX * P])
        WH = sb("w_high", [P, HRING, WMAX * P], F32R)
        WL = sb("w_low", [P, HRING, WMAX * P], F32R)
        X = sb("x_t", [P, KD, S])
        XH = sb("x_high", [P, KD, S], F32R)
        XL = sb("x_low", [P, KD, S], F32R)
        T = sb("tiles", [P, TT, S])
        R = sb("split_tiles", [P, RT, S], F32R)
        MAT = sb("mats", [P, len(CONSTS), P])
        M = {n: MAT[:, i, :] for i, n in enumerate(CONSTS)}
        mask = sb("mask", [P, 3 * P])
        diag = sb("diag", [P, P])
        zero = sb("zero", [P, 1])
        prm = sb("params", [P, 400])
        st = sb("stats", [P, 64])
        G = ctx.enter_context(nc.psum_tensor("gemm", [P, 2, S], F32))
        Q = ctx.enter_context(nc.psum_tensor("scores", [P, 4, S], F32))
        O = ctx.enter_context(nc.psum_tensor("outs", [P, 2, S], F32))

        names = ["w_taken", "w_split", "unit_done", "bank_free", "pe_to_dve", "dve_to_pe", "dve_to_act", "act_to_dve",
                 "act_to_pe", "dve_done", "act_done", "pool_done", "in_landed", "dve_to_sp", "out_stored",
                 "dve_to_pool", "rested", "pe_to_pool"]
        sem = {n: ctx.enter_context(nc.semaphore(n)) for n in names}
        w_landed = [ctx.enter_context(nc.semaphore(f"w_landed{i}")) for i in range(WRING)]
        for i, s_ in enumerate(w_landed):
            sem[f"w_landed{i}"] = s_

        class Engine:

            def __init__(self, kind, eng, waits):
                self.kind, self.eng, self.unit = kind, eng, 0
                self.sp, self.pool, self.act, self.dve, self.pe = (eng if kind == k else None for k in
                                                                   ("sp", "pool", "act", "dve", "pe"))
                self.seen = Seen(eng, kind, [(n, sem[n], 16 if "landed" in n or n == "out_stored" else 1)
                                             for n in waits])

            def rest(self):
                self.eng.sem_inc(sem["rested"], 1)

            def loop(self, n):
                self.rest()
                return self.eng.Fori(0, n)

        def pick(src, idx):
            return src[:, idx, :] if isinstance(idx, int) else src[:, ds(idx, 1), :]

        def unit(me, w, K, cols=P, src=None, bank=None, N=S, parts=1):
            s, h = me.unit % WRING, me.unit % HRING
            me.unit += 1
            n = K * cols
            if me.kind == "sp":
                me.eng.wait_ge(sem["w_taken"], me.seen("w_taken"))
                me.eng.dma_start(W32[:, s, 0:n].rearrange("p (k n) -> p k n", n=cols), w).then_inc(w_landed[s], 16)
            elif me.kind == "pool":
                me.eng.wait_ge(sem[f"w_landed{s}"], me.seen(f"w_landed{s}"))
                me.eng.wait_ge(sem["unit_done"], me.seen("unit_done"))
                me.eng.tensor_tensor(WH[:, h, 0:n], W32[:, s, 0:n], zero[:, 0:1].broadcast_to([P, n]),
                                     ALU.add).then_inc(sem["pool_done"], 1)
                me.eng.wait_ge(sem["pool_done"], me.seen("pool_done"))
                me.eng.tensor_tensor(WL[:, h, 0:n], W32[:, s, 0:n], WH[:, h, 0:n].bitcast(F32),
                                     ALU.subtract).then_inc(sem["pool_done"], 1)
                me.eng.wait_ge(sem["pool_done"], me.seen("pool_done"))
                me.eng.sem_inc(sem["w_taken"], 1)
                me.eng.sem_inc(sem["w_split"], 1)
            elif me.kind == "pe":
                me.seen(f"w_landed{s}")
                me.eng.wait_ge(sem["w_split"], me.seen("w_split"))
                me.eng.wait_ge(sem["bank_free"], me.seen("bank_free"))
                each = K // parts
                for part in range(parts):
                    o = (G[:, bank, :] if parts == 1 else Q[:, part, :])[0:cols, 0:N]
                    for k in range(each):
                        kk = part * each + k
                        hi, lo = src(kk)
                        wh = WH[:, h, kk * cols:(kk + 1) * cols]
                        wl = WL[:, h, kk * cols:(kk + 1) * cols]
                        me.eng.matmul(o, wh, hi, start=k == 0, stop=False)
                        me.eng.matmul(o, wh, lo, start=False, stop=False)
                        mm = me.eng.matmul(o, wl, hi, start=False, stop=k == each - 1)
                mm.then_inc(sem["unit_done"], 1)

        def gemm(me, w, K, iters, src, evac, N=S, body=4, cols=P):
            def once(i):
                for j in range(body):
                    if me.kind == "sp":
                        unit(me, w(i, j), K, cols)
                    elif me.kind in ("pool", "pe"):
                        unit(me, None, K, cols, src, j % 2, N)
                    elif me.kind == "dve":
                        me.eng.wait_ge(sem["unit_done"], me.seen("unit_done"))
                        evac(i, j, G[0:cols, j % 2, 0:N])
                        me.eng.sem_inc(sem["bank_free"], 1)
            if me.kind in ("sp", "pool", "pe", "dve"):
                if iters == 1:
                    once(0)
                else:
                    with me.loop(iters) as i:
                        once(i)

        def wcols(w, lead, k0, K, c0, cols=P):
            v = w if lead is None else w[ds(lead, 1)].rearrange("a r c -> (a r) c") if not isinstance(lead, int) \
                else w[lead]
            v = v[k0:k0 + K * P, c0:c0 + cols] if isinstance(c0, int) else v[k0:k0 + K * P, ds(c0, cols)]
            return v.rearrange("(k p) n -> p k n", p=P)

        def xs(k):
            return XH[:, k, :], XL[:, k, :]

        def split_tiles(me, z, hi, lo):
            if me.kind == "dve":
                me.eng.sem_inc(sem["dve_to_act"], 1)
                me.eng.wait_ge(sem["act_to_dve"], me.seen("act_to_dve"))
                me.eng.tensor_tensor(lo, z, hi.bitcast(F32), ALU.subtract).then_inc(sem["dve_done"], 1)
                me.eng.wait_ge(sem["dve_done"], me.seen("dve_done"))
            if me.kind == "act":
                me.eng.wait_ge(sem["dve_to_act"], me.seen("dve_to_act"))
                me.eng.activation(hi, z, ACT.Copy).then_inc(sem["act_done"], 1)
                me.eng.wait_ge(sem["act_done"], me.seen("act_done"))
                me.eng.sem_inc(sem["act_to_dve"], 1)

        def mm(me, o, l, r, start=True, stop=True):
            return me.eng.matmul(o, l, r, start=start, stop=stop)

        def dve(me, name, *args, **kw):
            if me.kind == "dve":
                fn = {"tt": me.eng.tensor_tensor, "ts": me.eng.tensor_scalar, "stt": me.eng.scalar_tensor_tensor,
                      "cp": me.eng.tensor_copy, "rec": me.eng.reciprocal, "max": me.eng.reduce_max}[name]
                fn(*args, **kw).then_inc(sem["dve_done"], 1)
                me.dve.wait_ge(sem["dve_done"], me.seen("dve_done"))

        def bc(ap, n):
            return ap.unsqueeze(1).broadcast_to([ap.shape[0], n, ap.shape[1]])

        def total(me, z, o, const, n):
            def calls():
                for k in range(n):
                    last = mm(me, o, const, z[:, k, :], k == 0, k == n - 1)
                return last
            if me.dve:
                me.dve.sem_inc(sem["dve_to_pe"], 1)
                me.dve.wait_ge(sem["pe_to_dve"], me.seen("pe_to_dve"))
            if me.pe:
                me.pe.wait_ge(sem["dve_to_pe"], me.seen("dve_to_pe"))
                calls().then_inc(sem["pe_to_dve"], 1)

        def rstd(me, src, dst, scale, eps):
            if me.dve:
                me.dve.tensor_scalar(dst, src, scale, eps, ALU.mult, ALU.add).then_inc(sem["dve_done"], 1)
                me.dve.wait_ge(sem["dve_done"], me.seen("dve_done"))
                me.dve.sem_inc(sem["dve_to_act"], 1)
                me.dve.wait_ge(sem["act_to_dve"], me.seen("act_to_dve"))
            if me.act:
                me.act.wait_ge(sem["dve_to_act"], me.seen("dve_to_act"))
                me.act.activation(dst, dst, ACT.Sqrt).then_inc(sem["act_done"], 1)
                me.act.wait_ge(sem["act_done"], me.seen("act_done"))
                me.act.sem_inc(sem["act_to_dve"], 1)
            if me.dve:
                me.dve.reciprocal(dst, dst).then_inc(sem["dve_done"], 1)
                me.dve.wait_ge(sem["dve_done"], me.seen("dve_done"))

        def norm(me, z, dst, g, b=None, sq=None, center=True, eps=1e-5, n=KD, ratio=1.0, parts=None):
            sq = T[:, 0:n, :] if sq is None else sq
            if center:
                total(me, z, O[:, 0, :], M["mean"], n)
                if me.dve:
                    me.dve.tensor_scalar(T[:, 21, :], O[:, 0, :], ratio, None, ALU.mult).then_inc(sem["dve_done"], 1)
                    me.dve.wait_ge(sem["dve_done"], me.seen("dve_done"))
            if me.kind == "dve":
                for k in range(n):
                    if center:
                        me.eng.tensor_tensor(z[:, k, :], z[:, k, :], T[:, 21, :],
                                             ALU.subtract).then_inc(sem["dve_done"], 1)
                        me.eng.wait_ge(sem["dve_done"], me.seen("dve_done"))
                    me.eng.sem_inc(sem["dve_to_act"], 1)
            if me.kind == "act":
                for k in range(n):
                    me.eng.wait_ge(sem["dve_to_act"], me.seen("dve_to_act"))
                    me.eng.activation(sq[:, k, :], z[:, k, :], ACT.Square).then_inc(sem["act_to_pe"], 1)
            if me.kind == "pe":
                for k in range(n):
                    me.eng.wait_ge(sem["act_to_pe"], me.seen("act_to_pe"))
                    last = mm(me, O[:, 0, :], M["mean"], sq[:, k, :], k == 0, k == n - 1)
                last.then_inc(sem["pe_to_dve"], 1)
            if me.kind == "dve":
                me.eng.wait_ge(sem["pe_to_dve"], me.seen("pe_to_dve"))
            rstd(me, O[:, 0, :], T[:, 21, :], ratio, eps)
            if me.kind == "dve":
                for k in range(n):
                    me.eng.tensor_tensor(dst[:, k, :], z[:, k, :], T[:, 21, :], ALU.mult).then_inc(sem["dve_done"], 1)
                    me.eng.wait_ge(sem["dve_done"], me.seen("dve_done"))
                    if g is not None:
                        me.eng.sem_inc(sem["dve_to_act"], 1)
            if me.kind == "act" and g is not None:
                for k in range(n):
                    me.eng.wait_ge(sem["dve_to_act"], me.seen("dve_to_act"))
                    bias = 0.0 if b is None else b[:, k:k + 1]
                    me.eng.activation(dst[:, k, :], dst[:, k, :], ACT.Identity, bias=bias,
                                      scale=g[:, k:k + 1]).then_inc(sem["act_done"], 1)
                    me.eng.wait_ge(sem["act_done"], me.seen("act_done"))
                    if parts is not None:
                        me.eng.activation(parts[0][:, k, :], dst[:, k, :], ACT.Copy).then_inc(sem["act_done"], 1)
                        me.eng.wait_ge(sem["act_done"], me.seen("act_done"))
                    me.eng.sem_inc(sem["act_to_dve"], 1)
            if me.kind == "dve" and g is not None:
                for k in range(n):
                    me.eng.wait_ge(sem["act_to_dve"], me.seen("act_to_dve"))
                    if parts is not None:
                        me.eng.tensor_tensor(parts[1][:, k, :], dst[:, k, :], parts[0][:, k, :].bitcast(F32),
                                             ALU.subtract).then_inc(sem["dve_done"], 1)
                        me.eng.wait_ge(sem["dve_done"], me.seen("dve_done"))

        def rope(me, t, n, rot, cos, sin, tmp):
            for k in range(n):
                if me.dve:
                    me.dve.sem_inc(sem["dve_to_pe"], 1)
                    me.dve.wait_ge(sem["pe_to_dve"], me.seen("pe_to_dve"))
                if me.pe:
                    me.pe.wait_ge(sem["dve_to_pe"], me.seen("dve_to_pe"))
                    mm(me, Q[:, 0, :], M[rot], t[:, k, :]).then_inc(sem["pe_to_dve"], 1)
                if me.dve:
                    me.dve.tensor_tensor(tmp, Q[:, 0, :], sin, ALU.mult).then_inc(sem["dve_done"], 1)
                    me.dve.wait_ge(sem["dve_done"], me.seen("dve_done"))
                    me.dve.tensor_tensor(t[:, k, :], t[:, k, :], cos, ALU.mult).then_inc(sem["dve_done"], 1)
                    me.dve.wait_ge(sem["dve_done"], me.seen("dve_done"))
                    me.dve.tensor_tensor(t[:, k, :], t[:, k, :], tmp, ALU.add).then_inc(sem["dve_done"], 1)
                    me.dve.wait_ge(sem["dve_done"], me.seen("dve_done"))

        def to_natural(me, src, dst, nb=NB):
            def calls():
                for c in range(nb):
                    last = me.eng.transpose(Q[:, 0, c * P:(c + 1) * P], src[:, c * P:(c + 1) * P], M["ident"])
                return last
            if me.dve:
                me.dve.sem_inc(sem["dve_to_pe"], 1)
                me.dve.wait_ge(sem["pe_to_dve"], me.seen("pe_to_dve"))
            if me.pe:
                me.pe.wait_ge(sem["dve_to_pe"], me.seen("dve_to_pe"))
                calls().then_inc(sem["pe_to_dve"], 1)
            if me.dve:
                me.dve.tensor_copy(dst,
                                   Q[:, 0, 0:nb * P].rearrange('p (c f) -> p c f', c=nb)).then_inc(sem["dve_done"], 1)
                me.dve.wait_ge(sem["dve_done"], me.seen("dve_done"))

        def softmax(me, maps, nk, scale, bias, pm, sink=None, nmap=4):
            mx, sm, sk = st[:, 0:nmap], st[:, 4:4 + nmap], st[:, 8:8 + nmap]
            p_ = pm[:, 0:nmap, 0:nk]
            logits, inner = (Q[:, :, 0:nk], scale) if bias is None else (pm[:, :, 0:nk], 1.0)
            if bias is not None:
                if me.dve:
                    me.dve.scalar_tensor_tensor(p_, Q[:, 0:nmap, 0:nk], scale, bias, ALU.mult,
                                                ALU.add).then_inc(sem["dve_done"], 1)
                    me.dve.wait_ge(sem["dve_done"], me.seen("dve_done"))
            if me.kind == "dve":
                me.eng.reduce_max(mx, logits[:, 0:nmap, :], AX).then_inc(sem["dve_done"], 1)
                me.eng.wait_ge(sem["dve_done"], me.seen("dve_done"))
                if sink is not None:
                    me.eng.tensor_tensor(mx, mx, sink, ALU.max).then_inc(sem["dve_done"], 1)
                    me.eng.wait_ge(sem["dve_done"], me.seen("dve_done"))
                    me.eng.tensor_tensor(sk, sink, mx, ALU.subtract).then_inc(sem["dve_done"], 1)
                    me.eng.wait_ge(sem["dve_done"], me.seen("dve_done"))
                me.eng.tensor_scalar(mx, mx, -inner, None, ALU.mult).then_inc(sem["dve_done"], 1)
                me.eng.wait_ge(sem["dve_done"], me.seen("dve_done"))
            calls = [((pm[:, m, 0:nk], logits[:, m, :], ACT.Exp),
                      dict(bias=mx[:, m:m + 1], scale=inner, accum_out=sm[:, m:m + 1]))
                     for m in range(nmap)]
            if sink is not None:
                calls.append(((sk, sk, ACT.Exp), {}))
            if me.dve:
                me.dve.sem_inc(sem["dve_to_act"], 1)
                me.dve.wait_ge(sem["act_to_dve"], me.seen("act_to_dve"))
            if me.act:
                me.act.wait_ge(sem["dve_to_act"], me.seen("dve_to_act"))
                for args, kw in calls:
                    me.act.activation(*args, **kw).then_inc(sem["act_done"], 1)
                    me.act.wait_ge(sem["act_done"], me.seen("act_done"))
                me.act.sem_inc(sem["act_to_dve"], 1)
            if me.kind == "dve":
                if sink is not None:
                    me.eng.tensor_tensor(sm, sm, sk, ALU.add).then_inc(sem["dve_done"], 1)
                    me.eng.wait_ge(sem["dve_done"], me.seen("dve_done"))
                me.eng.reciprocal(sm, sm).then_inc(sem["dve_done"], 1)
                me.eng.wait_ge(sem["dve_done"], me.seen("dve_done"))
                me.eng.tensor_tensor(p_, p_, sm.unsqueeze(2).broadcast_to([P, nmap, nk]),
                                     ALU.mult).then_inc(sem["dve_done"], 1)
                me.eng.wait_ge(sem["dve_done"], me.seen("dve_done"))

        def turn(me, pm, pt, nkb, nmap=4):
            def calls():
                for b in range(nkb):
                    for m in range(nmap):
                        last = me.eng.transpose(Q[:, b, m * P:(m + 1) * P], pm[:, m, b * P:(b + 1) * P], M["ident"])
                return last
            if me.dve:
                me.dve.sem_inc(sem["dve_to_pe"], 1)
                me.dve.wait_ge(sem["pe_to_dve"], me.seen("pe_to_dve"))
            if me.pe:
                me.pe.wait_ge(sem["dve_to_pe"], me.seen("dve_to_pe"))
                calls().then_inc(sem["pe_to_dve"], 1)
            if me.dve:
                me.dve.tensor_copy(pt[:, 0:nkb, 0:nmap * P], Q[:, 0:nkb, 0:nmap * P]).then_inc(sem["dve_done"], 1)
                me.dve.wait_ge(sem["dve_done"], me.seen("dve_done"))

        def gqa(me, qt, kdup, vn, first, nk_of, bias_of, sink, dst_h, dst_l, blk, g, fill=None):
            k0, nk = nk_of
            pm, pt = first
            def scores():
                for m in range(4):
                    b = 64 * (m % 2)
                    last = mm(me, Q[:, m, 0:nk], qt[b:b + 64, 2 * g + m // 2, blk * P:(blk + 1) * P],
                              kdup[b:b + 64, g, k0:k0 + nk])
                return last
            if me.dve:
                me.dve.sem_inc(sem["dve_to_pe"], 1)
                me.dve.wait_ge(sem["pe_to_dve"], me.seen("pe_to_dve"))
            if me.pe:
                me.pe.wait_ge(sem["dve_to_pe"], me.seen("dve_to_pe"))
                scores().then_inc(sem["pe_to_dve"], 1)
            if fill is not None and me.kind in ("sp", "pool", "pe"):
                fill(me)
            softmax(me, 4, nk, 0.125, bias_of, pm, sink)
            if fill is not None and me.kind == "dve":
                fill(me)
            turn(me, pm, pt, nk // P)
            def values():
                for odd in range(2):
                    for b in range(nk // P):
                        rhs = pt[:, b, :].rearrange("p (m q) -> p m q", m=4)[:, odd::2, :]
                        last = mm(me, O[64 * odd:64 * odd + 64, 0, 0:2 * P], vn[:, k0 // P + b, 64 * g:64 * g + 64],
                                  rhs, b == 0, b == nk // P - 1)
                return last
            if me.dve:
                me.dve.sem_inc(sem["dve_to_pe"], 1)
                me.dve.wait_ge(sem["pe_to_dve"], me.seen("pe_to_dve"))
            if me.pe:
                me.pe.wait_ge(sem["dve_to_pe"], me.seen("dve_to_pe"))
                values().then_inc(sem["pe_to_dve"], 1)
            o = O[:, 0, 0:2 * P].rearrange("p (m q) -> p m q", m=2)
            hi = dst_h[:, 2 * g:2 * g + 2, blk * P:(blk + 1) * P]
            lo = dst_l[:, 2 * g:2 * g + 2, blk * P:(blk + 1) * P]
            split_tiles(me, o, hi, lo)

        def load(me, *pairs):
            if me.kind == "dve":
                me.eng.sem_inc(sem["dve_to_sp"], 1)
                me.eng.wait_ge(sem["in_landed"], me.seen("in_landed", len(pairs)))
            if me.kind == "sp":
                me.eng.wait_ge(sem["dve_to_sp"], me.seen("dve_to_sp"))
                for dst, src in pairs:
                    with nc.allow_non_contiguous_dma(reason="small parameter columns"):
                        me.eng.dma_start(dst, src).then_inc(sem["in_landed"], 16)

        def lead(w, l):
            v = w[ds(l, 1)] if not isinstance(l, int) else w[l:l + 1]
            return v

        def cols_of(w, l, n):
            return lead(w, l).rearrange("a (t p) -> p (a t)", p=P) if n else None

        def dup_keys(me, src, dst):
            def calls():
                for g in range(2):
                    last = mm(me, Q[:, g, :], M[f"dup{g}"], src)
                return last
            if me.dve:
                me.dve.sem_inc(sem["dve_to_pe"], 1)
                me.dve.wait_ge(sem["pe_to_dve"], me.seen("pe_to_dve"))
            if me.pe:
                me.pe.wait_ge(sem["dve_to_pe"], me.seen("dve_to_pe"))
                calls().then_inc(sem["pe_to_dve"], 1)
            if me.dve:
                me.dve.tensor_copy(dst, Q[:, 0:2, :]).then_inc(sem["dve_done"], 1)
                me.dve.wait_ge(sem["dve_done"], me.seen("dve_done"))

        C = {}
        at = 0
        for n, w_ in (("b_gate", 24), ("c_ln_g", 4), ("c_ln_b", 4), ("ln1_g", 8), ("ln1_b", 8), ("ln2_g", 8),
                      ("ln2_b", 8), ("ln3_g", 8), ("ln3_b", 8), ("f_conv_b", 44), ("gains", 2), ("c_bs", 16),
                      ("sink", 8), ("conv_k", 132)):
            C[n] = prm[:, at:at + w_]
            at += w_
        assert at <= 400

        c_act = prm[:, 320:328]

        def modulate(l, first, count):
            def fill(me):
                for c in range(first, first + count):
                    s_ = me.unit % WRING
                    if me.kind in ("sp", "pool", "pe"):
                        me.unit += 1
                    if me.kind == "sp":
                        w = a["mod_w_2"][ds(l, 1)].rearrange("a w r c -> (a w) r c")[c // 24]
                        me.eng.wait_ge(sem["w_taken"], me.seen("w_taken"))
                        me.eng.dma_start(W32[:, s_, 0:KD * P].rearrange("p (k n) -> p k n", n=P),
                                         w[:, (c % 24) * P:(c % 24 + 1) * P].rearrange("(k p) n -> p k n", p=P)
                                         ).then_inc(w_landed[s_], 16)
                    elif me.kind == "pool":
                        me.seen(f"w_landed{s_}")
                    elif me.kind == "pe":
                        me.eng.wait_ge(sem[f"w_landed{s_}"], me.seen(f"w_landed{s_}"))
                        for k in range(KD):
                            last = mm(me, O[:, 1, ds(l * 48 + c, 1)], W32[:, s_, k * P:(k + 1) * P],
                                      c_act[:, k:k + 1], k == 0, k == KD - 1)
                        last.then_inc(sem["w_taken"], 1)
            return fill

        def first_layer(me, l):
            sp = me.kind == "sp"

            def c(n):
                return cols_of(a[n], l, 1) if sp else None
            load(me, *[(C[n], c(n)) for n in ("b_gate", "c_ln_g", "c_ln_b", "ln1_g", "ln1_b", "ln2_g", "ln2_b",
                                              "ln3_g", "ln3_b", "f_conv_b")],
                 *[(C["gains"][64 * h:64 * h + 64, q:q + 1],
                    lead(a[n], l).rearrange("a p -> p a") if sp else None)
                   for q, n in enumerate(("b_q_gain", "b_k_gain")) for h in range(2)],
                 (C["sink"], lead(a["a_sink"], l).broadcast_to([P, 8]) if sp else None),
                 *[(C["conv_k"][:, 44 * j:44 * j + 44],
                    lead(a["f_conv_k"], l)[:, j].rearrange("a (t p) -> p (a t)", p=P) if sp else None)
                   for j in range(3)],
                 (T[:, 20, :], a["ropes"][:, 0, :] if sp else None),
                 (T[:, 21, :], a["ropes"][:, 1, :] if sp else None))
            gemm(me, lambda i, j: wcols(a["w_in"], l, 0, KD, j * P), KD, 1, xs,
                 lambda i, j, o: dve(me, "cp", T[:, j, :], o), body=6)

            def project(first, count):
                def fill(me):
                    for n in range(first, min(first + count, 20)):
                        if sp:
                            unit(me, wcols(a["w_in"], l, 0, KD, n * P), KD)
                        elif me.kind in ("pool", "pe"):
                            unit(me, None, KD, src=xs, bank=n % 2)
                        elif me.kind == "dve":
                            me.eng.wait_ge(sem["unit_done"], me.seen("unit_done"))
                            me.eng.tensor_copy(T[:, n, :], G[:, n % 2, :]).then_inc(sem["dve_done"], 1)
                            me.eng.wait_ge(sem["dve_done"], me.seen("dve_done"))
                            me.eng.sem_inc(sem["bank_free"], 1)
                return fill
            pm, pt = T2[:, 0:4, :], T2[:, 4:8, :]
            rope(me, T[:, 0:5, :], 5, "rotA", T[:, 20, :], T[:, 21, :], T2[:, 0, :])
            dup_keys(me, T[:, 4, :], T[:, 20:22, :])
            to_natural(me, T[:, 5, :], T[:, 4, :].rearrange("p (c f) -> p c f", c=NB))
            vn = T[:, 4, :].rearrange("p (c f) -> p c f", c=NB)
            for g in range(2):
                for blk in range(NB):
                    lo_, hi_ = max(blk - 1, 0), min(blk + 2, NB)
                    nk = (hi_ - lo_) * P
                    mb = mask[:, (lo_ - blk + 1) * P:(lo_ - blk + 1) * P + nk]
                    gqa(me, T[:, 0:4, :], T[:, 20:22, :], vn, (pm, pt), (lo_ * P, nk), bc(mb, 4),
                        C["sink"][:, 4 * g:4 * g + 4], R[:, 0:4, :], R[:, 12:16, :], blk, g,
                        project(6 + 2 * (NB * g + blk), 2))
            load(me, (T[:, 20, :], a["ropes"][:, 2, :] if sp else None),
                 (T[:, 21, :], a["ropes"][:, 3, :] if sp else None))
            for k in range(5):
                t = T[:, 6 + k, :]
                if me.dve:
                    me.dve.sem_inc(sem["dve_to_act"], 1)
                    me.dve.wait_ge(sem["act_to_dve"], me.seen("act_to_dve"))
                if me.act:
                    me.act.wait_ge(sem["dve_to_act"], me.seen("dve_to_act"))
                    me.act.activation(T2[:, 0, :], t, ACT.Square).then_inc(sem["act_done"], 1)
                    me.act.wait_ge(sem["act_done"], me.seen("act_done"))
                    me.act.sem_inc(sem["act_to_dve"], 1)
                if me.dve:
                    me.dve.sem_inc(sem["dve_to_pe"], 1)
                    me.dve.wait_ge(sem["pe_to_dve"], me.seen("pe_to_dve"))
                if me.pe:
                    me.pe.wait_ge(sem["dve_to_pe"], me.seen("dve_to_pe"))
                    mm(me, Q[:, 0, :], M['pair'], T2[:, 0, :]).then_inc(sem["pe_to_dve"], 1)
                rstd(me, Q[:, 0, :], T2[:, 1, :], 1.0, 1e-6)
                gc = C["gains"][:, 0:1] if k < 4 else C["gains"][:, 1:2]
                if me.dve:
                    me.dve.scalar_tensor_tensor(t, t, gc, T2[:, 1, :], ALU.mult, ALU.mult).then_inc(sem["dve_done"], 1)
                    me.dve.wait_ge(sem["dve_done"], me.seen("dve_done"))
            rope(me, T[:, 6:11, :], 5, "rotB", T[:, 20, :], T[:, 21, :], T2[:, 0, :])
            dup_keys(me, T[:, 10, :], T[:, 20:22, :])
            to_natural(me, T[:, 11, :], vn)
            for g in range(2):
                for blk in range(NB):
                    gqa(me, T[:, 6:10, :], T[:, 20:22, :], vn, (pm, pt), (0, S), None, None,
                        R[:, 4:8, :], R[:, 16:20, :], blk, g, modulate(l, 6 * (NB * g + blk), 6))
            if me.kind == "pe":
                me.eng.drain().then_inc(sem["pe_to_pool"], 1)
            if me.kind == "pool":
                me.eng.wait_ge(sem["pe_to_pool"], me.seen("pe_to_pool"))
            if me.dve:
                me.dve.sem_inc(sem["dve_to_act"], 1)
                me.dve.wait_ge(sem["act_to_dve"], me.seen("act_to_dve"))
            if me.act:
                me.act.wait_ge(sem["dve_to_act"], me.seen("dve_to_act"))
                for k in range(12, 20):
                    me.act.activation(T[:, k, :], T[:, k, :], ACT.Gelu).then_inc(sem["act_done"], 1)
                    me.act.wait_ge(sem["act_done"], me.seen("act_done"))
                me.act.sem_inc(sem["act_to_dve"], 1)
            norm(me, T[:, 16:20, :], T[:, 16:20, :], C["c_ln_g"], C["c_ln_b"], sq=T[:, 0:4, :], n=4, ratio=2.0)
            load(me, (T[:, 1, :].rearrange("p (g j) -> p g j", g=4),
                      lead(a["c_ws"], l).rearrange("a g i j -> i (a g) j") if sp else None),
                 (T[:, 3, :], lead(a["c_bs"], l).rearrange("a g i -> a (g i)").broadcast_to([P, S]) if sp else None))
            to_natural(me, T[:, 1, :], T[:, 2, :].rearrange("p (c f) -> p c f", c=4))
            for g in range(4):
                to_natural(me, T[:, 16 + g, :], vn)
                def mix():
                    for c_ in range(NB):
                        last = mm(me, O[:, 0, c_ * P:(c_ + 1) * P], vn[:, c_, :], T[:, 2, g * P:(g + 1) * P])
                    return last
                if me.dve:
                    me.dve.sem_inc(sem["dve_to_pe"], 1)
                    me.dve.wait_ge(sem["pe_to_dve"], me.seen("pe_to_dve"))
                if me.pe:
                    me.pe.wait_ge(sem["dve_to_pe"], me.seen("dve_to_pe"))
                    mix().then_inc(sem["pe_to_dve"], 1)
                v3 = T2[:, 0, :].rearrange("p (c i) -> p c i", c=NB)
                if me.dve:
                    me.dve.tensor_tensor(v3, O[:, 0, :].rearrange('p (c i) -> p c i', c=NB),
                                         bc(T[:, 3, g * P:(g + 1) * P], NB), ALU.add).then_inc(sem["dve_done"], 1)
                    me.dve.wait_ge(sem["dve_done"], me.seen("dve_done"))
                    me.dve.tensor_tensor(T[:, 12 + g, :], T[:, 12 + g, :], T2[:, 0, :],
                                         ALU.mult).then_inc(sem["dve_done"], 1)
                    me.dve.wait_ge(sem["dve_done"], me.seen("dve_done"))
            split_tiles(me, T[:, 12:16, :], R[:, 8:12, :], R[:, 20:24, :])
            if me.kind in ("sp", "pool", "pe", "dve", "act"):
                with me.loop(KD) as d:
                    for n in range(3):
                        if sp:
                            unit(me, wcols(a["w_in"], l, 0, KD, GATE0 + n * D + d * P), KD)
                        elif me.kind in ("pe", "pool"):
                            unit(me, None, KD, src=xs, bank=n % 2)
                        elif me.kind == "dve":
                            me.eng.wait_ge(sem["unit_done"], me.seen("unit_done"))
                            me.eng.tensor_scalar(T2[:, n, :], G[:, n % 2, :], C['b_gate'][:, ds(d + n * KD, 1)], None,
                                                 ALU.add).then_inc(sem["dve_done"], 1)
                            me.eng.wait_ge(sem["dve_done"], me.seen("dve_done"))
                            me.eng.sem_inc(sem["bank_free"], 1)
                    if me.dve:
                        me.dve.sem_inc(sem["dve_to_act"], 1)
                        me.dve.wait_ge(sem["act_to_dve"], me.seen("act_to_dve"))
                    if me.act:
                        me.act.wait_ge(sem["dve_to_act"], me.seen("dve_to_act"))
                        me.act.activation(T2[:, 0:3, :], T2[:, 0:3, :], ACT.Sigmoid).then_inc(sem["act_done"], 1)
                        me.act.wait_ge(sem["act_done"], me.seen("act_done"))
                        me.act.sem_inc(sem["act_to_dve"], 1)
                    if sp:
                        unit(me, lead(a["w_branch"], l).rearrange("a n r c -> (a n r) c")[:, ds(d * P, P)]
                             .rearrange("(k p) n -> p k n", p=P), 12)
                    elif me.kind in ("pe", "pool"):
                        unit(me, None, 12, src=lambda k: (R[:, k, :], R[:, 12 + k, :]), parts=3)
                    elif me.kind == "dve":
                        me.eng.wait_ge(sem["unit_done"], me.seen("unit_done"))
                        me.eng.tensor_tensor(T2[:, 0:3, :], T2[:, 0:3, :], Q[:, 0:3, :],
                                             ALU.mult).then_inc(sem["dve_done"], 1)
                        me.eng.wait_ge(sem["dve_done"], me.seen("dve_done"))
                        me.eng.sem_inc(sem["bank_free"], 1)
                        me.eng.tensor_tensor(T2[:, 0, :], T2[:, 0, :], T2[:, 1, :],
                                             ALU.add).then_inc(sem["dve_done"], 1)
                        me.eng.wait_ge(sem["dve_done"], me.seen("dve_done"))
                        me.eng.tensor_tensor(T[:, ds(d, 1), :], T2[:, 0:1, :], T2[:, 2:3, :],
                                             ALU.add).then_inc(sem["dve_done"], 1)
                        me.eng.wait_ge(sem["dve_done"], me.seen("dve_done"))
            split_tiles(me, T[:, 0:8, :], XH[:], XL[:])
            residual = lambda i, j, o: dve(me, "stt", pick(X, i * 4 + j), pick(X, i * 4 + j), ALPHA,
                                           o if isinstance(i, int) else o.unsqueeze(1), ALU.mult, ALU.add)
            gemm(me, lambda i, j: wcols(a["w_mix_out"], l, 0, KD, i * 4 * P + j * P), KD, 2, handover(me, xs), residual)
            norm(me, X[:], X[:], C["ln1_g"], C["ln1_b"], parts=(XH, XL))
            load(me, (T[:, 0:4, :].rearrange("p (b k) n -> p b (k n)", b=2),
                      a["mem"][0].rearrange("(b p) n -> p b n", p=P) if sp else None))
            for k in range(KD):
                def mt():
                    for b in range(2):
                        last = me.eng.transpose(Q[:, 0, b * P:(b + 1) * P],
                                                T[:, 2 * b + k // 4, (k % 4) * P:(k % 4 + 1) * P], M["ident"])
                    return last
                if me.dve:
                    me.dve.sem_inc(sem["dve_to_pe"], 1)
                    me.dve.wait_ge(sem["pe_to_dve"], me.seen("pe_to_dve"))
                if me.pe:
                    me.pe.wait_ge(sem["dve_to_pe"], me.seen("dve_to_pe"))
                    mt().then_inc(sem["pe_to_dve"], 1)
                split_tiles(me, Q[:, 0, 0:MEM], R[:, k, 0:MEM], R[:, k, MEM:S])
            gemm(me, lambda i, j: wcols(a["x_wkv"], l, 0, KD, i * 4 * P + j * P), KD, 2,
                 handover(me, lambda k: (R[:, k, 0:MEM], R[:, k, MEM:S])),
                 lambda i, j, o: dve(me, "cp", T[:, ds(i * 4 + j + 4, 1), 0:MEM], o.unsqueeze(1)), N=MEM)
            gemm(me, lambda i, j: wcols(a["x_wq"], l, 0, KD, j * P), KD, 1, xs,
                 lambda i, j, o: dve(me, "cp", T[:, j, :], o))
            for h in range(4):
                to_natural(me, T[:, 8 + h, 0:MEM], T[:, 12 + h, 0:MEM].rearrange("p (c f) -> p c f", c=2), nb=2)
            for blk in range(NB):
                def xscore():
                    for m in range(4):
                        last = mm(me, Q[:, m, 0:MEM], T[:, m, blk * P:(blk + 1) * P], T[:, 4 + m, 0:MEM])
                    return last
                if me.dve:
                    me.dve.sem_inc(sem["dve_to_pe"], 1)
                    me.dve.wait_ge(sem["pe_to_dve"], me.seen("pe_to_dve"))
                if me.pe:
                    me.pe.wait_ge(sem["dve_to_pe"], me.seen("dve_to_pe"))
                    xscore().then_inc(sem["pe_to_dve"], 1)
                softmax(me, 4, MEM, P ** -0.5, None, pm)
                turn(me, pm, pt, 2)
                def xval():
                    for m in range(4):
                        for b in range(2):
                            last = mm(me, O[:, 0, m * P:(m + 1) * P], T[:, 12 + m, b * P:(b + 1) * P],
                                      pt[:, b, m * P:(m + 1) * P], b == 0, b == 1)
                    return last
                if me.dve:
                    me.dve.sem_inc(sem["dve_to_pe"], 1)
                    me.dve.wait_ge(sem["pe_to_dve"], me.seen("pe_to_dve"))
                if me.pe:
                    me.pe.wait_ge(sem["dve_to_pe"], me.seen("dve_to_pe"))
                    xval().then_inc(sem["pe_to_dve"], 1)
                split_tiles(me, O[:, 0, :].rearrange("p (m q) -> p m q", m=4), R[:, 0:4, blk * P:(blk + 1) * P],
                            R[:, 4:8, blk * P:(blk + 1) * P])
            gemm(me, lambda i, j: wcols(a["x_wo"], l, 0, 4, i * 4 * P + j * P), 4, 2,
                 handover(me, lambda k: (R[:, k, :], R[:, 4 + k, :])), residual)
            norm(me, X[:], X[:], C["ln2_g"], C["ln2_b"], parts=(XH, XL))
            if me.dve:
                me.dve.tensor_scalar(X[:], X[:], ALPHA, None, ALU.mult).then_inc(sem["dve_done"], 1)
                me.dve.wait_ge(sem["dve_done"], me.seen("dve_done"))
            t0 = 0
            for nt in (8, 8, 6):
                def w_up(i, j):
                    return wcols(a["f_w_up"], l, 0, KD, t0 * P + i * 2 * P + (j // 2) * P + (j % 2) * D_FF)

                def conv(i, j, o):
                    if me.kind == "act":
                        return
                    acc = T2[:, j % 2, :]
                    tile = i * 2 + j // 2 + t0 + (j % 2) * (D_FF // P)
                    kc = [C["conv_k"][:, ds(tile + 44 * q, 1)] for q in range(3)]
                    me.eng.tensor_scalar(acc, o, kc[1], C['f_conv_b'][:, ds(tile, 1)], ALU.mult,
                                         ALU.add).then_inc(sem["dve_done"], 1)
                    me.eng.wait_ge(sem["dve_done"], me.seen("dve_done"))
                    me.eng.scalar_tensor_tensor(acc[:, 1:S], o[:, 0:S - 1], kc[0], acc[:, 1:S], ALU.mult,
                                                ALU.add).then_inc(sem["dve_done"], 1)
                    me.eng.wait_ge(sem["dve_done"], me.seen("dve_done"))
                    me.eng.scalar_tensor_tensor(acc[:, 0:S - 1], o[:, 1:S], kc[2], acc[:, 0:S - 1], ALU.mult,
                                                ALU.add).then_inc(sem["dve_done"], 1)
                    me.eng.wait_ge(sem["dve_done"], me.seen("dve_done"))
                if me.kind in ("sp", "pool", "pe", "dve", "act"):
                    if me.kind == "pe":
                        me.eng.wait_ge(sem["dve_to_pe"], me.seen("dve_to_pe"))
                    if me.kind == "dve":
                        me.eng.sem_inc(sem["dve_to_pe"], 1)
                    with me.loop(nt // 2) as i:
                        for j in range(4):
                            if sp:
                                unit(me, w_up(i, j), KD)
                            elif me.kind in ("pool", "pe"):
                                unit(me, None, KD, src=xs, bank=j % 2)
                            elif me.kind == "dve":
                                me.eng.wait_ge(sem["unit_done"], me.seen("unit_done"))
                                conv(i, j, G[:, j % 2, :])
                                me.eng.sem_inc(sem["bank_free"], 1)
                            if j % 2:
                                if me.dve:
                                    me.dve.sem_inc(sem["dve_to_act"], 1)
                                    me.dve.wait_ge(sem["act_to_dve"], me.seen("act_to_dve"))
                                if me.act:
                                    me.act.wait_ge(sem["dve_to_act"], me.seen("dve_to_act"))
                                    me.act.activation(T2[:, 0, :], T2[:, 0, :], ACT.Gelu).then_inc(sem["act_done"], 1)
                                    me.act.wait_ge(sem["act_done"], me.seen("act_done"))
                                    me.act.sem_inc(sem["act_to_dve"], 1)
                                q = i * 2 + j // 2
                                if me.dve:
                                    me.dve.tensor_tensor(T[:, ds(q, 1), :], T2[:, 0:1, :], T2[:, 1:2, :],
                                                         ALU.mult).then_inc(sem["dve_done"], 1)
                                    me.dve.wait_ge(sem["dve_done"], me.seen("dve_done"))
                split_tiles(me, T[:, 0:nt, :], R[:, 0:nt, :], R[:, 8:8 + nt, :])
                gemm(me, lambda i, j: wcols(a["f_w_down"], l, t0 * P, nt, i * 4 * P + j * P), nt, 2,
                     handover(me, lambda k: (R[:, k, :], R[:, 8 + k, :])),
                     lambda i, j, o: dve(me, "tt", pick(X, i * 4 + j), pick(X, i * 4 + j), o.unsqueeze(1), ALU.add))
                t0 += nt
            norm(me, X[:], X[:], C["ln3_g"], C["ln3_b"], parts=(XH, XL))
            sync_pe(me)

        T2 = sb("work", [P, 8, S])

        def sync_pe(me):
            if me.kind == "dve":
                me.eng.sem_inc(sem["dve_to_pe"], 1)
            if me.kind == "pe":
                me.eng.wait_ge(sem["dve_to_pe"], me.seen("dve_to_pe"))

        def handover(me, src):
            sync_pe(me)
            return src

        md_all = prm[:, 200:296]
        md, gc, pc = prm[:, 8:32], prm[:, 32:64], prm[:, 64:200]
        Y = T[:, 8:16, :]

        def colsp(ap):
            return ap.rearrange("(t p) -> p t", p=P)

        def modulation(me, layer, which):
            load(me, (gc[:, 0:24], colsp(a["mod_b_2"][layer, which])),
                 (gc[:, 24:32], colsp(a["norm_gains_2"][layer, 2 * which])))
            n = 48 * layer + 24 * which
            if me.dve:
                me.dve.tensor_tensor(md, md_all[:, n:n + 24], gc[:, 0:24], ALU.add).then_inc(sem["dve_done"], 1)
                me.dve.wait_ge(sem["dve_done"], me.seen("dve_done"))
                me.dve.scalar_tensor_tensor(gc[:, 0:8], md[:, 8:16], 1.0, gc[:, 24:32], ALU.add,
                                            ALU.mult).then_inc(sem["dve_done"], 1)
                me.dve.wait_ge(sem["dve_done"], me.seen("dve_done"))
            load(me, (gc[:, 24:32], colsp(a["norm_gains_2"][layer, 2 * which + 1])))
            if me.dve:
                me.dve.tensor_tensor(gc[:, 8:16], md[:, 16:24], gc[:, 24:32], ALU.mult).then_inc(sem["dve_done"], 1)
                me.dve.wait_ge(sem["dve_done"], me.seen("dve_done"))

        def sandwich_in(me, layer, which):
            modulation(me, layer, which)
            norm(me, X[:], T[:, 0:8, :], gc[:, 0:8], md[:, 0:8], sq=T[:, 8:16, :], center=False, eps=1e-6,
                 parts=(XH, XL))
            sync_pe(me)

        def sandwich_out(me):
            norm(me, Y, Y, gc[:, 8:16], sq=T[:, 0:8, :], center=False, eps=1e-6)
            if me.dve:
                me.dve.tensor_tensor(X[:], X[:], Y, ALU.add).then_inc(sem["dve_done"], 1)
                me.dve.wait_ge(sem["dve_done"], me.seen("dve_done"))

        def add_to_y(i, j, o):
            if cur[0].dve:
                cur[0].dve.tensor_tensor(pick(T, i * 4 + j + 8), pick(T, i * 4 + j + 8), o.unsqueeze(1),
                                         ALU.add).then_inc(sem["dve_done"], 1)
                cur[0].dve.wait_ge(sem["dve_done"], cur[0].seen("dve_done"))

        def set_y(i, j, o):
            if cur[0].dve:
                cur[0].dve.tensor_copy(pick(T, i * 4 + j + 8), o.unsqueeze(1)).then_inc(sem["dve_done"], 1)
                cur[0].dve.wait_ge(sem["dve_done"], cur[0].seen("dve_done"))

        cur = [None]

        def mlp(me, layer):
            w1, w2 = a["mlp_w1_2"][layer], a["mlp_w2_2"][layer]
            if me.kind == "dve":
                me.eng.memset(Y, 0.0).then_inc(sem["dve_done"], 1)
                me.eng.wait_ge(sem["dve_done"], me.seen("dve_done"))

            def relu2(i, j, o):
                if me.dve:
                    me.dve.tensor_scalar(T2[:, 0, :], o, 0.0, None, ALU.max).then_inc(sem["dve_done"], 1)
                    me.dve.wait_ge(sem["dve_done"], me.seen("dve_done"))
                    me.dve.tensor_tensor(T[:, ds(i * 4 + j, 1), :], T2[:, 0:1, :], T2[:, 0:1, :],
                                         ALU.mult).then_inc(sem["dve_done"], 1)
                    me.dve.wait_ge(sem["dve_done"], me.seen("dve_done"))
            with me.loop(4) as ck:
                sync_pe(me)
                gemm(me, lambda i, j: w1[:, ds(ck * D + i * 4 * P + j * P, P)].rearrange("(k p) n -> p k n", p=P),
                     KD, 2, xs, relu2)
                split_tiles(me, T[:, 0:8, :], R[:, 0:8, :], R[:, 8:16, :])
                gemm(me, lambda i, j: w2[ds(ck * D, D), ds(i * 4 * P + j * P, P)]
                     .rearrange("(k p) n -> p k n", p=P), KD, 2,
                     handover(me, lambda k: (R[:, k, :], R[:, 8 + k, :])), add_to_y)

        def causal_blocks():
            return [(cs, cl) for cs in range(NB) for cl in range(cs, NB)]

        def ssd(me):
            w = a["e_w_in_2"][0]
            sp = me.kind == "sp"
            cw, cb_, dtb, alog, dsk, gn = (pc[:, 0:64], pc[:, 64:80], pc[:, 80:81], pc[:, 81:82], pc[:, 82:90],
                                           pc[:, 90:98])
            load(me, *[(cw[:, 16 * j:16 * j + 16], colsp(a["e_conv_w_2"][0, j])) for j in range(4)],
                 (cb_, colsp(a["e_conv_b_2"][0])), (dtb[0:16, :], a["e_dt_bias_2"][0:1].rearrange("a h -> h a")),
                 (alog[0:16, :], a["e_A_log_2"][0:1].rearrange("a h -> h a")),
                 *[(dsk[64 * h:64 * h + 64, :], a["e_D_2"][0:1, h::2].broadcast_to([64, 8])) for h in range(2)],
                 (gn, colsp(a["e_ssd_norm_2"][0])))

            def conv(i, j, o):
                t = T[:, ds(i * 4 + j, 1), :]
                kc = [cw[:, ds(i * 4 + j + 16 * q, 1)] for q in range(4)]
                o3 = o.unsqueeze(1)
                if me.dve:
                    me.dve.tensor_scalar(t, o3, kc[3], cb_[:, ds(i * 4 + j, 1)], ALU.mult,
                                         ALU.add).then_inc(sem["dve_done"], 1)
                    me.dve.wait_ge(sem["dve_done"], me.seen("dve_done"))
                for d in (1, 2, 3):
                    if me.dve:
                        me.dve.scalar_tensor_tensor(t[:, :, d:S], o3[:, :, 0:S - d], kc[3 - d], t[:, :, d:S], ALU.mult,
                                                    ALU.add).then_inc(sem["dve_done"], 1)
                        me.dve.wait_ge(sem["dve_done"], me.seen("dve_done"))
            gemm(me, lambda i, j: w[:, ds(i * 4 * P + j * P + D, P)].rearrange("(k p) n -> p k n", p=P), KD, 4, xs,
                 conv)
            if me.dve:
                me.dve.sem_inc(sem["dve_to_act"], 1)
                me.dve.wait_ge(sem["act_to_dve"], me.seen("act_to_dve"))
            if me.act:
                me.act.wait_ge(sem["dve_to_act"], me.seen("dve_to_act"))
                me.act.activation(T[:, 0:16, :], T[:, 0:16, :], ACT.Silu).then_inc(sem["act_done"], 1)
                me.act.wait_ge(sem["act_done"], me.seen("act_done"))
                me.act.sem_inc(sem["act_to_dve"], 1)
            dtT, dAT, acsT = T2[0:16, 0, :], T2[0:16, 1, :], T2[0:16, 3, :]
            gemm(me, lambda i, j: w[j * 512:(j + 1) * 512, 3 * D:3 * D + 16].rearrange("(k p) n -> p k n", p=P), 4, 1,
                 None, lambda i, j, o: dve(me, "cp", T2[0:16, j, :], o), body=2, cols=16) if me.kind != "pe" else \
                [unit(me, None, 4, 16, (lambda k, j=j: xs(4 * j + k)), j) for j in range(2)]
            if me.dve:
                me.dve.scalar_tensor_tensor(dtT, T2[0:16, 1, :], dtb[0:16, 0:1], dtT, ALU.add,
                                            ALU.add).then_inc(sem["dve_done"], 1)
                me.dve.wait_ge(sem["dve_done"], me.seen("dve_done"))
            if me.dve:
                me.dve.tensor_scalar(T2[0:16, 1, :], dtT, -1.0, None, ALU.mult).then_inc(sem["dve_done"], 1)
                me.dve.wait_ge(sem["dve_done"], me.seen("dve_done"))
                me.dve.tensor_tensor(T2[0:16, 1, :], dtT, T2[0:16, 1, :], ALU.min).then_inc(sem["dve_done"], 1)
                me.dve.wait_ge(sem["dve_done"], me.seen("dve_done"))
                me.dve.sem_inc(sem["dve_to_act"], 1)
                me.dve.wait_ge(sem["act_to_dve"], me.seen("act_to_dve"))
            if me.act:
                me.act.wait_ge(sem["dve_to_act"], me.seen("dve_to_act"))
                me.act.activation(T2[0:16, 1, :], T2[0:16, 1, :], ACT.Exp).then_inc(sem["act_done"], 1)
                me.act.wait_ge(sem["act_done"], me.seen("act_done"))
                me.act.activation(alog[0:16, :], alog[0:16, :], ACT.Exp).then_inc(sem["act_done"], 1)
                me.act.wait_ge(sem["act_done"], me.seen("act_done"))
                me.act.sem_inc(sem["act_to_dve"], 1)
            if me.dve:
                me.dve.tensor_scalar(T2[0:16, 1, :], T2[0:16, 1, :], 1.0, None, ALU.add).then_inc(sem["dve_done"], 1)
                me.dve.wait_ge(sem["dve_done"], me.seen("dve_done"))
                me.dve.sem_inc(sem["dve_to_act"], 1)
                me.dve.wait_ge(sem["act_to_dve"], me.seen("act_to_dve"))
            if me.act:
                me.act.wait_ge(sem["dve_to_act"], me.seen("dve_to_act"))
                me.act.activation(T2[0:16, 1, :], T2[0:16, 1, :], ACT.Ln).then_inc(sem["act_done"], 1)
                me.act.wait_ge(sem["act_done"], me.seen("act_done"))
                me.act.sem_inc(sem["act_to_dve"], 1)
            if me.dve:
                me.dve.scalar_tensor_tensor(dtT, dtT, 0.0, T2[0:16, 1, :], ALU.max,
                                            ALU.add).then_inc(sem["dve_done"], 1)
                me.dve.wait_ge(sem["dve_done"], me.seen("dve_done"))
                me.dve.tensor_scalar(dAT, dtT, alog[0:16, 0:1], -1.0, ALU.mult, ALU.mult).then_inc(sem["dve_done"], 1)
                me.dve.wait_ge(sem["dve_done"], me.seen("dve_done"))
            nat = T2[:, 2, :]
            dtN, dAN, acsN, tot = (nat[:, 64 * q:64 * q + 64] for q in range(4))

            def flip():
                for q in range(2):
                    for c in range(NB):
                        last = me.eng.transpose(Q[:, 0, 64 * q + 16 * c:64 * q + 16 * c + 16],
                                                T2[0:16, q, c * P:(c + 1) * P], M["ident"][0:16, 0:16])
                return last
            if me.dve:
                me.dve.sem_inc(sem["dve_to_pe"], 1)
                me.dve.wait_ge(sem["pe_to_dve"], me.seen("pe_to_dve"))
            if me.pe:
                me.pe.wait_ge(sem["dve_to_pe"], me.seen("dve_to_pe"))
                me.rest()
                flip().then_inc(sem["pe_to_dve"], 1)
            if me.dve:
                me.dve.tensor_copy(nat[:, 0:128], Q[:, 0, 0:128]).then_inc(sem["dve_done"], 1)
                me.dve.wait_ge(sem["dve_done"], me.seen("dve_done"))

            def sums():
                mm(me, Q[:, 0, 0:64], M["tri"], dAN)
                mm(me, Q[:, 1, 0:64], M["ones"], dAN)
                for c in range(NB):
                    last = mm(me, Q[0:16, 2, c * P:(c + 1) * P], dAN[:, 16 * c:16 * c + 16], M["tri"])
                return last
            if me.dve:
                me.dve.sem_inc(sem["dve_to_pe"], 1)
                me.dve.wait_ge(sem["pe_to_dve"], me.seen("pe_to_dve"))
            if me.pe:
                me.pe.wait_ge(sem["dve_to_pe"], me.seen("dve_to_pe"))
                sums().then_inc(sem["pe_to_dve"], 1)
            if me.dve:
                me.dve.tensor_copy(acsN, Q[:, 0, 0:64]).then_inc(sem["dve_done"], 1)
                me.dve.wait_ge(sem["dve_done"], me.seen("dve_done"))
                me.dve.tensor_copy(tot, Q[:, 1, 0:64]).then_inc(sem["dve_done"], 1)
                me.dve.wait_ge(sem["dve_done"], me.seen("dve_done"))
                me.dve.tensor_copy(acsT, Q[0:16, 2, :]).then_inc(sem["dve_done"], 1)
                me.dve.wait_ge(sem["dve_done"], me.seen("dve_done"))
            pairs = causal_blocks()

            def cbias(n):
                return nat[:, 256 + 16 * n:256 + 16 * n + 16]
            for n, (cs, cl) in enumerate(pairs):
                if cs == cl:
                    if me.dve:
                        me.dve.tensor_scalar(cbias(n), acsN[:, 16 * cs:16 * cs + 16], -1.0, None,
                                             ALU.mult).then_inc(sem["dve_done"], 1)
                        me.dve.wait_ge(sem["dve_done"], me.seen("dve_done"))
                else:
                    if me.dve:
                        me.dve.tensor_tensor(cbias(n), cbias(n - 1), tot[:, 16 * (cl - 1):16 * cl],
                                             ALU.add).then_inc(sem["dve_done"], 1)
                        me.dve.wait_ge(sem["dve_done"], me.seen("dve_done"))
            CBm, E = T[:, 16:20, :], T2[:, 4:8, :]
            xn = T[:, 20, :].rearrange("p (c f) -> p c f", c=NB)
            cbg, dtg = st[:, 16:56], st[:, 0:16]
            with me.loop(4) as g:
                if me.dve:
                    me.dve.tensor_copy(E[:, 0:1, :], T[:, ds(g + 8, 1), :]).then_inc(sem["dve_done"], 1)
                    me.dve.wait_ge(sem["dve_done"], me.seen("dve_done"))
                    me.dve.tensor_copy(E[:, 1:2, :], T[:, ds(g + 12, 1), :]).then_inc(sem["dve_done"], 1)
                    me.dve.wait_ge(sem["dve_done"], me.seen("dve_done"))

                def cb():
                    for cs in range(NB):
                        last = mm(me, Q[:, cs, cs * P:S], E[:, 0, cs * P:(cs + 1) * P], E[:, 1, cs * P:S])
                    return last
                if me.dve:
                    me.dve.sem_inc(sem["dve_to_pe"], 1)
                    me.dve.wait_ge(sem["pe_to_dve"], me.seen("pe_to_dve"))
                if me.pe:
                    me.pe.wait_ge(sem["dve_to_pe"], me.seen("dve_to_pe"))
                    cb().then_inc(sem["pe_to_dve"], 1)
                for cs in range(NB):
                    if me.dve:
                        me.dve.tensor_copy(CBm[:, cs, cs * P:S], Q[:, cs, cs * P:S]).then_inc(sem["dve_done"], 1)
                        me.dve.wait_ge(sem["dve_done"], me.seen("dve_done"))
                if me.dve:
                    me.dve.tensor_copy(cbg.rearrange('p (n h) -> p n h', h=4),
                                       nat[:, 256:416].rearrange('p (n h) -> p n h', h=16)[:, :, ds(g * 4, 4)]).then_inc(sem["dve_done"], 1)
                    me.dve.wait_ge(sem["dve_done"], me.seen("dve_done"))
                    me.dve.tensor_copy(dtg.rearrange('p (c h) -> p c h', h=4),
                                       dtN.rearrange('p (c h) -> p c h', h=16)[:, :, ds(g * 4, 4)]).then_inc(sem["dve_done"], 1)
                    me.dve.wait_ge(sem["dve_done"], me.seen("dve_done"))
                for t in range(2):
                    if me.dve:
                        me.dve.tensor_copy(E[:, 0:1, :], T[:, ds(g * 2 + t, 1), :]).then_inc(sem["dve_done"], 1)
                        me.dve.wait_ge(sem["dve_done"], me.seen("dve_done"))
                    to_natural(me, E[:, 0, :], xn)
                    for hh in range(2):
                        xh = xn[:, :, 64 * hh:64 * hh + 64]
                        h4 = 2 * t + hh
                        if me.dve:
                            me.dve.tensor_tensor(xh, xh,
                                                 dtg.rearrange('p (c h) -> p c h', h=4)[:, :, h4:h4 + 1].broadcast_to([P, NB, 64]),
                                                 ALU.mult).then_inc(sem["dve_done"], 1)
                            me.dve.wait_ge(sem["dve_done"], me.seen("dve_done"))
                            me.dve.tensor_scalar(T2[0:16, 0, :], acsT, M['ident'][0:16, ds(g * 4 + h4, 1)], None,
                                                 ALU.mult).then_inc(sem["dve_done"], 1)
                            me.dve.wait_ge(sem["dve_done"], me.seen("dve_done"))
                            me.dve.sem_inc(sem["dve_to_pe"], 1)
                            me.dve.wait_ge(sem["pe_to_dve"], me.seen("pe_to_dve"))
                        if me.pe:
                            me.pe.wait_ge(sem["dve_to_pe"], me.seen("dve_to_pe"))
                            mm(me, O[:, 0, :], M['ones'][0:16, :], T2[0:16, 0, :]).then_inc(sem["pe_to_dve"], 1)
                        if me.dve:
                            me.dve.tensor_tensor(T2[:, 1, :].rearrange('p (c l) -> p c l', c=NB),
                                                 O[:, 0, :].rearrange('p (c l) -> p c l', c=NB), bc(diag[:], NB),
                                                 ALU.add).then_inc(sem["dve_done"], 1)
                            me.dve.wait_ge(sem["dve_done"], me.seen("dve_done"))
                            me.dve.sem_inc(sem["dve_to_act"], 1)
                            me.dve.wait_ge(sem["act_to_dve"], me.seen("act_to_dve"))
                        if me.act:
                            me.act.wait_ge(sem["dve_to_act"], me.seen("dve_to_act"))
                            for (n, (cs, cl)) in enumerate(pairs):
                                me.act.activation(E[:, cs, cl * P:(cl + 1) * P],
                                                  (T2[:, 1, :] if cs == cl else O[:, 0, :])[:, cl * P:(cl + 1) * P],
                                                  ACT.Exp,
                                                  bias=cbg[:, 4 * n + h4:4 * n + h4 + 1]).then_inc(sem["act_done"], 1)
                                me.act.wait_ge(sem["act_done"], me.seen("act_done"))
                            me.act.sem_inc(sem["act_to_dve"], 1)
                        for cs in range(NB):
                            if me.dve:
                                me.dve.tensor_tensor(E[:, cs, cs * P:S], E[:, cs, cs * P:S], CBm[:, cs, cs * P:S],
                                                     ALU.mult).then_inc(sem["dve_done"], 1)
                                me.dve.wait_ge(sem["dve_done"], me.seen("dve_done"))

                        def ys():
                            for cs in range(NB):
                                last = mm(me, O[64 * hh:64 * hh + 64, 1, cs * P:S], xn[:, cs, 64 * hh:64 * hh + 64],
                                          E[:, cs, cs * P:S], cs == 0, cs == NB - 1)
                            return last
                        if me.dve:
                            me.dve.sem_inc(sem["dve_to_pe"], 1)
                            me.dve.wait_ge(sem["pe_to_dve"], me.seen("pe_to_dve"))
                        if me.pe:
                            me.pe.wait_ge(sem["dve_to_pe"], me.seen("dve_to_pe"))
                            ys().then_inc(sem["pe_to_dve"], 1)
                    xt = T[:, ds(g * 2 + t, 1), :]
                    if me.dve:
                        me.dve.scalar_tensor_tensor(xt, xt, dsk[:, ds(g * 2 + t, 1)], O[:, 1:2, :], ALU.mult,
                                                    ALU.add).then_inc(sem["dve_done"], 1)
                        me.dve.wait_ge(sem["dve_done"], me.seen("dve_done"))
            gemm(me, lambda i, j: w[:, ds(i * 4 * P + j * P, P)].rearrange("(k p) n -> p k n", p=P), KD, 2, xs, set_y)
            if me.dve:
                me.dve.sem_inc(sem["dve_to_act"], 1)
                me.dve.wait_ge(sem["act_to_dve"], me.seen("act_to_dve"))
            if me.act:
                me.act.wait_ge(sem["dve_to_act"], me.seen("dve_to_act"))
                me.act.activation(Y, Y, ACT.Silu).then_inc(sem["act_done"], 1)
                me.act.wait_ge(sem["act_done"], me.seen("act_done"))
                me.act.sem_inc(sem["act_to_dve"], 1)
            if me.dve:
                me.dve.tensor_tensor(T[:, 0:8, :], T[:, 0:8, :], Y, ALU.mult).then_inc(sem["dve_done"], 1)
                me.dve.wait_ge(sem["dve_done"], me.seen("dve_done"))
            norm(me, T[:, 0:8, :], T[:, 0:8, :], gn, sq=Y, center=False, eps=1e-6,
                 parts=(R[:, 0:8, :], R[:, 8:16, :]))
            gemm(me, lambda i, j: a["e_w_out_2"][0, 0:D, ds(i * 4 * P + j * P, P)]
                 .rearrange("(k p) n -> p k n", p=P), KD, 2, handover(me, lambda k: (R[:, k, :], R[:, 8 + k, :])),
                 set_y)

        def bias_rows(me):
            sp = me.kind == "sp"
            load(me, (T2[0:32, 0, 0:8], a["rel_bias_2"]), (T2[0:32, 1:3, 0:320],
                                                           a["onehot"].rearrange("b (a x) -> b a x", a=2)),
                 *[(T2[0:8, 3 + 2 * v:5 + 2 * v, 0:320], a["bmask"][v].rearrange("b (a x) -> b a x", a=2))
                   for v in range(2)])

            def rows():
                for v in range(2):
                    last = mm(me, Q[0:8, v, 0:320], T2[0:32, 0, 0:8], T2[0:32, 1 + v, 0:320])
                return last
            if me.dve:
                me.dve.sem_inc(sem["dve_to_pe"], 1)
                me.dve.wait_ge(sem["pe_to_dve"], me.seen("pe_to_dve"))
            if me.pe:
                me.pe.wait_ge(sem["dve_to_pe"], me.seen("dve_to_pe"))
                me.rest()
                rows().then_inc(sem["pe_to_dve"], 1)
            for v in range(2):
                if me.dve:
                    me.dve.tensor_tensor(T2[0:8, 3 + 2 * v:5 + 2 * v, 0:320], Q[0:8, 0:2, 0:320],
                                         T2[0:8, 3 + 2 * v:5 + 2 * v, 0:320], ALU.add).then_inc(sem["dve_done"], 1)
                    me.dve.wait_ge(sem["dve_done"], me.seen("dve_done"))
            load(me, *[(bias_dram[v].rearrange("b (a x) -> b a x", a=2), T2[0:8, 3 + 2 * v:5 + 2 * v, 0:320])
                       for v in range(2)])

        def toeplitz(me, tiles, v, heads, off, n):
            def hankel(h):
                r = bias_dram[v, ds(h, 1)] if not isinstance(h, int) else bias_dram[v, h:h + 1]
                return bass.AP(r.tensor, r.offset + off, [[1, P], [1, n]])
            load(me, *[(tiles[:, m, 0:n], hankel(h) if me.kind == "sp" else None) for m, h in enumerate(heads)])

            def turned():
                for m in range(len(heads)):
                    last = mm(me, Q[:, m, 0:n], M["flip"], tiles[:, m, 0:n])
                return last
            if me.dve:
                me.dve.sem_inc(sem["dve_to_pe"], 1)
                me.dve.wait_ge(sem["pe_to_dve"], me.seen("pe_to_dve"))
            if me.pe:
                me.pe.wait_ge(sem["dve_to_pe"], me.seen("dve_to_pe"))
                turned().then_inc(sem["pe_to_dve"], 1)
            if me.dve:
                me.dve.tensor_copy(tiles[:, 0:len(heads), 0:n], Q[:, 0:len(heads), 0:n]).then_inc(sem["dve_done"], 1)
                me.dve.wait_ge(sem["dve_done"], me.seen("dve_done"))

        def diff(me):
            w = a["e_w_in_2"][0]
            sp = me.kind == "sp"
            lam, lr, sub = pc[:, 0:1], T2[:, 0, 0:256], pc[:, 8:9]
            load(me, (lr, a["e_lambda_2"][0:1].rearrange("a r d -> a (r d)").broadcast_to([P, 256])),
                 (sub, a["e_diff_norm_2"][0:1].rearrange("a p -> p a")))
            for q in range(2):
                if me.dve:
                    me.dve.tensor_tensor(lr[:, 128 * q:128 * q + 64], lr[:, 128 * q:128 * q + 64],
                                         lr[:, 128 * q + 64:128 * q + 128], ALU.mult).then_inc(sem["dve_done"], 1)
                    me.dve.wait_ge(sem["dve_done"], me.seen("dve_done"))
                if me.kind == "dve":
                    me.eng.reduce_sum(pc[:, q:q + 1], lr[:, 128 * q:128 * q + 64], AX).then_inc(sem["dve_done"], 1)
                    me.eng.wait_ge(sem["dve_done"], me.seen("dve_done"))
            if me.dve:
                me.dve.sem_inc(sem["dve_to_act"], 1)
                me.dve.wait_ge(sem["act_to_dve"], me.seen("act_to_dve"))
            if me.act:
                me.act.wait_ge(sem["dve_to_act"], me.seen("dve_to_act"))
                me.act.activation(pc[:, 0:2], pc[:, 0:2], ACT.Exp).then_inc(sem["act_done"], 1)
                me.act.wait_ge(sem["act_done"], me.seen("act_done"))
                me.act.sem_inc(sem["act_to_dve"], 1)
            if me.dve:
                me.dve.tensor_scalar(pc[:, 2:3], pc[:, 1:2], 1.0, -LAM_INIT, ALU.mult,
                                     ALU.add).then_inc(sem["dve_done"], 1)
                me.dve.wait_ge(sem["dve_done"], me.seen("dve_done"))
                me.dve.tensor_tensor(pc[:, 3:4], pc[:, 2:3], pc[:, 0:1], ALU.subtract).then_inc(sem["dve_done"], 1)
                me.dve.wait_ge(sem["dve_done"], me.seen("dve_done"))
                me.dve.tensor_scalar(sub, sub, 1.0 - LAM_INIT, None, ALU.mult).then_inc(sem["dve_done"], 1)
                me.dve.wait_ge(sem["dve_done"], me.seen("dve_done"))
            pm, pt = T2[:, 0:4, :], T2[:, 4:8, :]
            vn = T[:, 3, :].rearrange("p (c f) -> p c f", c=NB)
            q0 = 3 * D + 16

            def project(me, head, hh, which):
                for n in which:
                    bank = (3 * hh + n) % 2
                    if me.kind == "sp":
                        unit(me, w[:, head(q0 + n * D)].rearrange("(k p) n -> p k n", p=P), KD)
                    elif me.kind in ("pool", "pe"):
                        unit(me, None, KD, src=xs, bank=bank)
                    elif me.kind == "dve":
                        me.eng.wait_ge(sem["unit_done"], me.seen("unit_done"))
                        me.eng.tensor_copy(T[:, (0, 17)[hh] + n, :], G[:, bank, :]).then_inc(sem["dve_done"], 1)
                        me.eng.wait_ge(sem["dve_done"], me.seen("dve_done"))
                        me.eng.sem_inc(sem["bank_free"], 1)

            def pair(hp, last_pair):
                def head(i):
                    return lambda c: (slice(hp * 2 * P + c + i * P, hp * 2 * P + c + (i + 1) * P)
                                      if isinstance(hp, int) else ds(hp * 2 * P + (c + i * P), P))
                for hh in range(2):
                    h = hp * 2 + hh
                    q_, k_, v_ = (T[:, (0, 17)[hh] + n, :] for n in range(3))
                    toeplitz(me, T[:, 4:5, :], 0, [h], 0, S)
                    to_natural(me, v_, vn)
                    for blk in range(NB):
                        nk = (blk + 1) * P
                        more = blk < 3 and not (last_pair and hh == 1)

                        def scores():
                            for m in range(2):
                                last = mm(me, Q[:, m, 0:nk], q_[64 * m:64 * m + 64, blk * P:(blk + 1) * P],
                                          k_[64 * m:64 * m + 64, 0:nk])
                            return last
                        if me.dve:
                            me.dve.sem_inc(sem["dve_to_pe"], 1)
                            me.dve.wait_ge(sem["pe_to_dve"], me.seen("pe_to_dve"))
                        if me.pe:
                            me.pe.wait_ge(sem["dve_to_pe"], me.seen("dve_to_pe"))
                            scores().then_inc(sem["pe_to_dve"], 1)
                        if more and me.kind in ("sp", "pool", "pe"):
                            project(me, head(hh + 1), 1 - hh, [blk])
                        softmax(me, 2, nk, 0.125, bc(T[:, 4, S - nk:S], 2), pm, nmap=2)
                        if more and me.kind == "dve":
                            project(me, head(hh + 1), 1 - hh, [blk])
                        if me.dve:
                            me.dve.scalar_tensor_tensor(pm[:, 0, 0:nk], pm[:, 1, 0:nk], pc[:, 3:4], pm[:, 0, 0:nk],
                                                        ALU.mult, ALU.add).then_inc(sem["dve_done"], 1)
                            me.dve.wait_ge(sem["dve_done"], me.seen("dve_done"))
                        turn(me, pm, pt, blk + 1, nmap=1)

                        def values():
                            for b in range(blk + 1):
                                last = mm(me, O[:, 0, blk * P:(blk + 1) * P], vn[:, b, :], pt[:, b, 0:P], b == 0,
                                          b == blk)
                            return last
                        if me.dve:
                            me.dve.sem_inc(sem["dve_to_pe"], 1)
                            me.dve.wait_ge(sem["pe_to_dve"], me.seen("pe_to_dve"))
                        if me.pe:
                            me.pe.wait_ge(sem["dve_to_pe"], me.seen("dve_to_pe"))
                            values().then_inc(sem["pe_to_dve"], 1)
                        if me.dve:
                            me.dve.tensor_copy(T[:, 5, blk * P:(blk + 1) * P],
                                               O[:, 0, blk * P:(blk + 1) * P]).then_inc(sem["dve_done"], 1)
                            me.dve.wait_ge(sem["dve_done"], me.seen("dve_done"))
                    norm(me, T[:, 5:6, :], T[:, 5:6, :], sub, sq=T[:, 6:7, :], center=False, eps=1e-6, n=1, ratio=8.0)
                    hi, lo = ((R[:, h:h + 1, :], R[:, h + 8:h + 9, :]) if isinstance(h, int)
                              else (R[:, ds(h, 1), :], R[:, ds(h + 8, 1), :]))
                    split_tiles(me, T[:, 5:6, :], hi, lo)
            project(me, lambda c: slice(c, c + P), 0, range(3))
            with me.loop(3) as hp:
                pair(hp, False)
            pair(3, True)
            gemm(me, lambda i, j: a["e_w_out_2"][0, D:2 * D, ds(i * 4 * P + j * P, P)]
                 .rearrange("(k p) n -> p k n", p=P), KD, 2, handover(me, lambda k: (R[:, k, :], R[:, 8 + k, :])),
                 add_to_y)

        def retention(me):
            w = a["o_w_in_2"][0]
            sp = me.kind == "sp"
            load(me, (T[:, 18, :], a["ropes"][:, 4, :]), (T[:, 19, :], a["ropes"][:, 5, :]))
            E = T2[:, 4:8, :]
            vn = T[:, 6:8, :].rearrange("p e (c f) -> p e c f", c=NB)

            def project(me, hp, i, which):
                for n in which:
                    size = P if n < 2 else 2 * P
                    c0 = [0, 512, 1024, 1024 + P, 2048, 2048 + P][n] + i * size
                    if me.kind == "sp":
                        col = slice(hp * 2 * size + c0, hp * 2 * size + c0 + P) if isinstance(hp, int) \
                            else ds(hp * 2 * size + c0, P)
                        unit(me, w[:, col].rearrange("(k p) n -> p k n", p=P), KD)
                    elif me.kind in ("pool", "pe"):
                        unit(me, None, KD, src=xs, bank=n % 2)
                    elif me.kind == "dve":
                        me.eng.wait_ge(sem["unit_done"], me.seen("unit_done"))
                        me.eng.tensor_copy(T[:, 8 * (i % 2) + n, :], G[:, n % 2, :]).then_inc(sem["dve_done"], 1)
                        me.eng.wait_ge(sem["dve_done"], me.seen("dve_done"))
                        me.eng.sem_inc(sem["bank_free"], 1)

            def pair(hp, last_pair):
                for i in range(2):
                    B = 8 * i
                    load(me, (T[:, 17:18, :], (a["decay"][ds(hp * 2 + i, 1)] if not isinstance(hp, int)
                                               else a["decay"][2 * hp + i:2 * hp + i + 1]).rearrange("a p n -> p a n")
                              if sp else None))
                    rope(me, T[:, B:B + 2, :], 2, "rotC", T[:, 18, :], T[:, 19, :], T2[:, 0, :])
                    for e in range(2):
                        to_natural(me, T[:, B + 2 + e, :], vn[:, e])
                    more = not (last_pair and i == 1)

                    def scores():
                        for cs in range(NB):
                            last = mm(me, Q[:, cs, cs * P:S], T[:, B + 1, cs * P:(cs + 1) * P], T[:, B, cs * P:S])
                        return last
                    if me.dve:
                        me.dve.sem_inc(sem["dve_to_pe"], 1)
                        me.dve.wait_ge(sem["pe_to_dve"], me.seen("pe_to_dve"))
                    if me.pe:
                        me.pe.wait_ge(sem["dve_to_pe"], me.seen("dve_to_pe"))
                        scores().then_inc(sem["pe_to_dve"], 1)
                    for cs in range(NB):
                        if me.dve:
                            me.dve.scalar_tensor_tensor(E[:, cs, cs * P:S], Q[:, cs, cs * P:S], P ** (-0.5),
                                                        T[:, 17, 0:S - cs * P], ALU.mult,
                                                        ALU.mult).then_inc(sem["dve_done"], 1)
                            me.dve.wait_ge(sem["dve_done"], me.seen("dve_done"))

                    def values():
                        for e in range(2):
                            for cs in range(NB):
                                last = mm(me, O[:, e, cs * P:S], vn[:, e, cs, :], E[:, cs, cs * P:S], cs == 0,
                                          cs == NB - 1)
                        return last
                    if me.dve:
                        me.dve.sem_inc(sem["dve_to_pe"], 1)
                        me.dve.wait_ge(sem["pe_to_dve"], me.seen("pe_to_dve"))
                    if me.pe:
                        me.pe.wait_ge(sem["dve_to_pe"], me.seen("dve_to_pe"))
                        values().then_inc(sem["pe_to_dve"], 1)
                    if me.dve:
                        me.dve.tensor_copy(T2[:, 0:2, :], O[:]).then_inc(sem["dve_done"], 1)
                        me.dve.wait_ge(sem["dve_done"], me.seen("dve_done"))
                    norm(me, T2[:, 0:2, :], T2[:, 0:2, :], None, sq=T2[:, 2:4, :], center=False, eps=1e-6, n=2,
                         ratio=4.0)
                    if more and me.kind in ("sp", "pool", "pe"):
                        project(me, hp, i + 1, range(6))
                    if me.dve:
                        me.dve.sem_inc(sem["dve_to_act"], 1)
                        me.dve.wait_ge(sem["act_to_dve"], me.seen("act_to_dve"))
                    if me.act:
                        me.act.wait_ge(sem["dve_to_act"], me.seen("dve_to_act"))
                        me.act.activation(T[:, B + 4:B + 6, :], T[:, B + 4:B + 6, :],
                                          ACT.Silu).then_inc(sem["act_done"], 1)
                        me.act.wait_ge(sem["act_done"], me.seen("act_done"))
                        me.act.sem_inc(sem["act_to_dve"], 1)
                    if me.dve:
                        me.dve.tensor_tensor(T2[:, 0:2, :], T2[:, 0:2, :], T[:, B + 4:B + 6, :],
                                             ALU.mult).then_inc(sem["dve_done"], 1)
                        me.dve.wait_ge(sem["dve_done"], me.seen("dve_done"))
                    at_ = hp * 4 + 2 * i
                    hi, lo = ((R[:, at_:at_ + 2, :], R[:, at_ + 12:at_ + 14, :]) if isinstance(hp, int)
                              else (R[:, ds(at_, 2), :], R[:, ds(at_ + 12, 2), :]))
                    split_tiles(me, T2[:, 0:2, :], hi, lo)
                    if more and me.kind == "dve":
                        project(me, hp, i + 1, range(6))
            project(me, 0, 0, range(6))
            pair(0, False)
            pair(1, True)

        def sliding(me):
            w = a["o_w_in_2"][0]
            sp = me.kind == "sp"
            gemm(me, lambda i, j: w[:, 3 * D + j * P:3 * D + (j + 1) * P].rearrange("(k p) n -> p k n", p=P), KD, 1,
                 xs, lambda i, j, o: dve(me, "cp", T[:, j, :], o), body=6)
            sk = pc[:, 0:8]
            load(me, (sk, a["o_sinks_2"].broadcast_to([P, 8])))
            dup_keys(me, T[:, 4, :], T[:, 20:22, :])
            vn = T[:, 4, :].rearrange("p (c f) -> p c f", c=NB)
            to_natural(me, T[:, 5, :], vn)
            pm, pt = T2[:, 0:4, :], T2[:, 4:8, :]
            for g in range(2):
                toeplitz(me, T[:, 16:20, :], 1, range(4 * g, 4 * g + 4), 256, 256)
                for blk in range(NB):
                    k0 = max(blk - 1, 0)
                    nk = (blk + 1 - k0) * P
                    gqa(me, T[:, 0:4, :], T[:, 20:22, :], vn, (pm, pt), (k0 * P, nk), T[:, 16:20, 256 - nk:256],
                        sk[:, 4 * g:4 * g + 4], R[:, 8:12, :], R[:, 20:24, :], blk, g)
            gemm(me, lambda i, j: a["o_w_out_2"][0][:, ds(i * 4 * P + j * P, P)]
                 .rearrange("(k p) n -> p k n", p=P), 12, 2, handover(me, lambda k: (R[:, k, :], R[:, 12 + k, :])),
                 set_y)

        def from_second(me):
            cur[0] = me
            if me.dve:
                me.dve.tensor_copy(md_all, O[:, 1, 0:96]).then_inc(sem["dve_done"], 1)
                me.dve.wait_ge(sem["dve_done"], me.seen("dve_done"))
            bias_rows(me)
            sandwich_in(me, 0, 0)
            ssd(me)
            diff(me)
            sandwich_out(me)
            sandwich_in(me, 0, 1)
            mlp(me, 0)
            sandwich_out(me)
            sandwich_in(me, 1, 0)
            retention(me)
            sliding(me)
            sandwich_out(me)
            sandwich_in(me, 1, 1)
            mlp(me, 1)
            sandwich_out(me)

        def program(me):
            sp = me.kind == "sp"
            if me.kind == "dve":
                me.eng.memset(zero[:], 0.0).then_inc(sem["dve_done"], 1)
                me.eng.wait_ge(sem["dve_done"], me.seen("dve_done"))
                me.eng.sem_inc(sem["dve_to_pool"], 1)
                me.eng.sem_inc(sem["w_taken"], WRING)
                me.eng.sem_inc(sem["bank_free"], 2)
            if me.kind == "pool":
                me.eng.wait_ge(sem["dve_to_pool"], me.seen("dve_to_pool"))
            if me.kind == "pe":
                me.eng.sem_inc(sem["unit_done"], 2)
            if me.kind == "dve":
                me.eng.wait_ge(sem["unit_done"], me.seen("unit_done", 2))
            load(me, (MAT[:], a["mats"] if sp else None), (mask[:], a["band"] if sp else None),
                 (diag[:], a["diag"] if sp else None), (c_act, a["c_2"][0].rearrange("(t p) -> p t", p=P)),
                 (T[:, 0:8, :].rearrange("p (b k) n -> p b (k n)", b=NB),
                  a["x"][0].rearrange("(b p) n -> p b n", p=P) if sp else None))
            if me.dve:
                me.dve.sem_inc(sem["dve_to_act"], 1)
                me.dve.wait_ge(sem["act_to_dve"], me.seen("act_to_dve"))
            if me.act:
                me.act.wait_ge(sem["dve_to_act"], me.seen("dve_to_act"))
                me.act.activation(c_act, c_act, ACT.Silu).then_inc(sem["act_done"], 1)
                me.act.wait_ge(sem["act_done"], me.seen("act_done"))
                me.act.sem_inc(sem["act_to_dve"], 1)
            for k in range(KD):
                def xt():
                    for b in range(NB):
                        last = me.eng.transpose(Q[:, 0, b * P:(b + 1) * P],
                                                T[:, 2 * b + k // 4, (k % 4) * P:(k % 4 + 1) * P], M["ident"])
                    return last
                if me.dve:
                    me.dve.sem_inc(sem["dve_to_pe"], 1)
                    me.dve.wait_ge(sem["pe_to_dve"], me.seen("pe_to_dve"))
                if me.pe:
                    me.pe.wait_ge(sem["dve_to_pe"], me.seen("dve_to_pe"))
                    xt().then_inc(sem["pe_to_dve"], 1)
                if me.dve:
                    me.dve.tensor_copy(X[:, k, :], Q[:, 0, :]).then_inc(sem["dve_done"], 1)
                    me.dve.wait_ge(sem["dve_done"], me.seen("dve_done"))
            split_tiles(me, X[:], XH[:], XL[:])
            sync_pe(me)
            if me.kind == "sp" or True:
                with me.loop(DEPTH) as l:
                    first_layer(me, l)
            from_second(me)
            for b in range(NB):
                def ot():
                    for k in range(KD):
                        last = me.eng.transpose(Q[:, k // 4, (k % 4) * P:(k % 4 + 1) * P],
                                                X[:, k, b * P:(b + 1) * P], M["ident"])
                    return last
                if me.dve:
                    me.dve.sem_inc(sem["dve_to_pe"], 1)
                    me.dve.wait_ge(sem["pe_to_dve"], me.seen("pe_to_dve"))
                if me.pe:
                    me.pe.wait_ge(sem["dve_to_pe"], me.seen("dve_to_pe"))
                    ot().then_inc(sem["pe_to_dve"], 1)
                if me.dve:
                    me.dve.tensor_copy(T[:, 2 * b:2 * b + 2, :], Q[:, 0:2, :]).then_inc(sem["dve_done"], 1)
                    me.dve.wait_ge(sem["dve_done"], me.seen("dve_done"))
            if me.kind == "dve":
                me.eng.sem_inc(sem["dve_to_sp"], 1)
            if sp:
                me.eng.wait_ge(sem["dve_to_sp"], me.seen("dve_to_sp"))
                me.eng.dma_start(out[0].rearrange("(b p) n -> p b n", p=P),
                                 T[:, 0:8, :].rearrange("p (b k) n -> p b (k n)", b=NB)).then_inc(sem["out_stored"], 16)
                me.eng.wait_ge(sem["out_stored"], me.seen("out_stored"))
                me.rest()

        block = ctx.enter_context(nc.Block())

        @block.sync
        def _(eng):
            program(Engine("sp", eng, ["w_taken", "dve_to_sp", "out_stored"]))

        @block.gpsimd
        def _(eng):
            program(Engine("pool", eng, [f"w_landed{i}" for i in range(WRING)] + ["unit_done", "pool_done", "dve_to_pool", "pe_to_pool"]))

        @block.scalar
        def _(eng):
            program(Engine("act", eng, ["dve_to_act", "act_done"]))

        @block.vector
        def _(eng):
            program(Engine("dve", eng, ["unit_done", "pe_to_dve", "act_to_dve", "dve_done", "in_landed",
                                        "out_stored"]))

        @block.tensor
        def _(eng):
            program(Engine("pe", eng, ["w_landed0", "w_landed1", "w_split", "bank_free", "dve_to_pe",
                                      "act_to_pe"]))


_INS = ["x", "mem", "w_in", "b_gate", "a_sink", "b_q_gain", "b_k_gain", "c_ln_g", "c_ln_b", "c_ws", "c_bs",
        "w_branch", "w_mix_out", "ln1_g", "ln1_b", "x_wq", "x_wkv", "x_wo", "ln2_g", "ln2_b", "f_w_up", "f_conv_k",
        "f_conv_b", "f_w_down", "ln3_g", "ln3_b", "c_2", "rel_bias_2", "norm_gains_2", "mod_w_2", "mod_b_2",
        "mlp_w1_2", "mlp_w2_2", "e_w_in_2", "e_conv_w_2", "e_conv_b_2", "e_dt_bias_2", "e_A_log_2", "e_D_2",
        "e_ssd_norm_2", "e_lambda_2", "e_diff_norm_2", "e_w_out_2", "o_w_in_2", "o_sinks_2", "o_w_out_2"]


def kernel(**inputs):
    import concourse.bacc as _bacc
    from concourse import mybir as _mybir
    from concourse.bass_utils import run_bass_kernel_spmd as _run

    nc = _bacc.Bacc("TRN2", target_bir_lowering=False, num_devices=1)
    arrays, args = {}, {}
    given = {n: np.ascontiguousarray(inputs[n]) for n in _INS}
    given.update(constants())
    for name, v in given.items():
        arrays[f"in_{name}"] = v
        args[name] = nc.dram_tensor(f"in_{name}", v.shape, _mybir.dt.from_np(v.dtype), kind="ExternalInput").ap()
    out = nc.dram_tensor("out_0", (1, S, D), F32, kind="ExternalOutput").ap()
    scratch = nc.dram_tensor("bias_rows", (2, 8, 640), F32, kind="Internal").ap()
    build(nc, args, out, scratch)
    r = _run(nc, [arrays], core_ids=[0])
    return r.results[0]["out_0"]
```
